# Optimizing a Trainium2 kernel written in Bass

```python
import math
import jax, jax.numpy as jnp
from jax import lax
import numpy as np

D_MODEL = 1024
BATCH = 1
SEQ = 512
DEPTH = 2

N_HEADS_A = 8
HEAD_DIM_A = 64
WIDTH_A = N_HEADS_A * HEAD_DIM_A
DILATED_PATTERNS = ((128, 1), (512, 4), (2048, 16))
N_POOL_GROUPS = 4
POOL_WINDOWS = (2, 4, 8, 16)
WIDTH_B = D_MODEL // 2
POOL_GROUP_DIM = WIDTH_B // N_POOL_GROUPS
MIX_WIDTH_EVEN = WIDTH_A + WIDTH_B
IN_WIDTH_EVEN = 3 * WIDTH_A + WIDTH_B
REL_BUCKETS = 32
REL_MAX_DISTANCE = 2048
N_HEADS_C = 4
INNER_C = 2 * D_MODEL
HEAD_DIM_C = INNER_C // N_HEADS_C
CONV_WIDTH = 4
QKV_BLOCK = 4
MLSTM_CHUNK = 64
D_FF = 256 * ((8 * D_MODEL // 3 + 255) // 256)
FFN_RESIDUAL = 0.5
RMS_EPS = 1e-6
N_EVEN = (DEPTH + 1) // 2
N_ODD = DEPTH // 2

kernel_name = 'hybrid_dilated_pool_mlstm_macaron'

def rms_norm(x, gain):
    xf = x.astype(jnp.float32)
    y = xf * lax.rsqrt(jnp.mean(xf * xf, axis=-1, keepdims=True) + RMS_EPS)
    return (y * gain.astype(jnp.float32)).astype(x.dtype)

def swiglu(x, w_gate, w_up, w_down):
    return (jax.nn.silu(x @ w_gate) * (x @ w_up)) @ w_down

def t5_bucket(distance):
    max_exact = REL_BUCKETS // 2
    d = jnp.maximum(distance.astype(jnp.float32), 1.0)
    large = max_exact + (jnp.log(d / max_exact) / math.log(REL_MAX_DISTANCE / max_exact)
                         * (REL_BUCKETS - max_exact)).astype(jnp.int32)
    large = jnp.minimum(large, REL_BUCKETS - 1)
    return jnp.where(distance < max_exact, distance, large)

def dilated_band_attention(q, k, v, rel_bias, window, dilation):
    b, s, h, e = q.shape
    steps = window // dilation
    blk = steps
    span = dilation * blk
    s_pad = -(-s // span) * span
    n_sub = s_pad // dilation
    nb = n_sub // blk

    def to_blocks(t):
        t = jnp.pad(t, ((0, 0), (0, s_pad - s), (0, 0), (0, 0)))
        t = t.reshape(b, n_sub, dilation, h, e).transpose(0, 2, 3, 1, 4)
        return t.reshape(b, dilation, h, nb, blk, e)

    def with_prev(t):
        prev = jnp.pad(t, ((0, 0), (0, 0), (0, 0), (1, 0), (0, 0), (0, 0)))[:, :, :, :nb]
        return jnp.concatenate([prev, t], axis=4)

    def from_blocks(t):
        rest = t.shape[5:]
        t = jnp.moveaxis(t.reshape(b, dilation, h, n_sub, *rest), 3, 1)
        return t.reshape(b, s_pad, h, *rest)[:, :s]

    qb, kb, vb = to_blocks(q), to_blocks(k), to_blocks(v)
    kw, vw = with_prev(kb), with_prev(vb)
    kj = jnp.arange(2 * blk)[None, :]
    delta = (jnp.arange(blk)[:, None] + blk) - kj
    band = (delta >= 0) & (delta <= steps)
    valid = band[None] & ((jnp.arange(nb)[:, None, None] > 0) | (kj >= blk)[None])
    bias = rel_bias[t5_bucket(jnp.maximum(delta, 0) * dilation)].astype(jnp.float32)
    bias = jnp.transpose(bias, (2, 0, 1))[None, None, :, None]
    logits = jnp.einsum('bdhnqe,bdhnke->bdhnqk', qb, kw) + bias
    logits = jnp.where(valid[None, None, None], logits, -jnp.inf)
    m = jnp.max(logits, axis=-1, keepdims=True)
    p = jnp.exp(logits - m)
    denom = jnp.sum(p, axis=-1, keepdims=True)
    o = jnp.einsum('bdhnqk,bdhnke->bdhnqe', p, vw) / denom
    lse = (m + jnp.log(denom))[..., 0]
    return from_blocks(o), from_blocks(lse)

def multi_scale_pool(u, pool_w, pool_scale):
    b, s, _ = u.shape
    uf = u.astype(jnp.float32).reshape(b, s, N_POOL_GROUPS, POOL_GROUP_DIM)
    cs = jnp.cumsum(uf, axis=1)
    pos = jnp.arange(1, s + 1, dtype=jnp.float32)
    diffs = []
    for g, w in enumerate(POOL_WINDOWS):
        c = cs[:, :, g]
        lagged = jnp.pad(c, ((0, 0), (w, 0), (0, 0)))[:, :s]
        mean = (c - lagged) / jnp.minimum(pos, float(w))[:, None]
        diffs.append(mean - uf[:, :, g])
    y = jnp.einsum('bsgc,gcd->bsgd', jnp.stack(diffs, axis=2), pool_w.astype(jnp.float32))
    y = y.reshape(b, s, WIDTH_B) * pool_scale.astype(jnp.float32)
    return y.astype(u.dtype)

def dilated_pool_mixer(xn, rel_bias, w_in, q_gain, k_gain, pool_w, pool_scale, w_out):
    b, s, _ = xn.shape
    proj = xn @ w_in
    q, k, v, u = jnp.split(proj, [WIDTH_A, 2 * WIDTH_A, 3 * WIDTH_A], axis=-1)
    heads = lambda t: t.reshape(b, s, N_HEADS_A, HEAD_DIM_A).astype(jnp.float32)
    q = rms_norm(heads(q), q_gain) * HEAD_DIM_A ** -0.5
    k = rms_norm(heads(k), k_gain)
    v = heads(v)
    outs, lses = [], []
    for window, dilation in DILATED_PATTERNS:
        o, lse = dilated_band_attention(q, k, v, rel_bias, window, dilation)
        outs.append(o)
        lses.append(lse)
    wts = jax.nn.softmax(jnp.stack(lses), axis=0)
    attn = jnp.sum(wts[..., None] * jnp.stack(outs), axis=0).reshape(b, s, WIDTH_A)
    pooled = multi_scale_pool(u, pool_w, pool_scale)
    mixed = jnp.concatenate([attn.astype(xn.dtype), pooled], axis=-1)
    return mixed @ w_out

def mlstm_chunkwise(q, k, v, ig, fg):
    b, h, s, e = q.shape
    L = MLSTM_CHUNK
    nc = -(-s // L)
    pad = nc * L - s
    pad4 = lambda t: jnp.pad(t, ((0, 0), (0, 0), (0, pad), (0, 0)))
    pad3 = lambda t: jnp.pad(t, ((0, 0), (0, 0), (0, pad)))
    chunks = lambda t: jnp.moveaxis(t.reshape(b, h, nc, L, *t.shape[3:]), 2, 0)
    qc, kc, vc = chunks(pad4(q)), chunks(pad4(k)), chunks(pad4(v))
    ic = chunks(pad3(ig))
    bcum = jnp.cumsum(chunks(pad3(jax.nn.log_sigmoid(fg))), axis=-1)
    causal = jnp.tril(jnp.ones((L, L), dtype=bool))
    d_intra = jnp.where(causal, bcum[..., :, None] - bcum[..., None, :] + ic[..., None, :], -jnp.inf)
    b_last = bcum[..., -1]
    a_state = b_last[..., None] - bcum + ic

    def step(carry, xs):
        C, n, m = carry
        q_, k_, v_, dm, bc, a, bl = xs
        inter = bc + m[..., None]
        m_t = jnp.maximum(inter, jnp.max(dm, axis=-1))
        w_inter = jnp.exp(inter - m_t)
        s_qk = jnp.einsum('bhte,bhse->bhts', q_, k_) * jnp.exp(dm - m_t[..., None])
        num = (w_inter[..., None] * jnp.einsum('bhte,bhef->bhtf', q_, C)
               + jnp.einsum('bhts,bhsf->bhtf', s_qk, v_))
        den = w_inter * jnp.einsum('bhte,bhe->bht', q_, n) + jnp.sum(s_qk, axis=-1)
        h_out = num / jnp.maximum(jnp.abs(den), jnp.exp(-m_t))[..., None]
        m_new = jnp.maximum(bl + m, jnp.max(a, axis=-1))
        decay = jnp.exp(bl + m - m_new)
        w_s = jnp.exp(a - m_new[..., None])
        C = decay[..., None, None] * C + jnp.einsum('bhse,bhsf->bhef', k_ * w_s[..., None], v_)
        n = decay[..., None] * n + jnp.einsum('bhs,bhse->bhe', w_s, k_)
        return (C, n, m_new), h_out

    init = (jnp.zeros((b, h, e, e), jnp.float32), jnp.zeros((b, h, e), jnp.float32),
            jnp.zeros((b, h), jnp.float32))
    _, hs = lax.scan(step, init, (qc, kc, vc, d_intra, bcum, a_state, b_last))
    return jnp.moveaxis(hs, 0, 2).reshape(b, h, nc * L, e)[:, :, :s]

def mlstm_mixer(xn, w_in, conv_w, conv_b, wq, wk, wv, w_gates, b_gates, skip, out_gain, w_out):
    b, s, _ = xn.shape
    x_m, z = jnp.split(xn @ w_in, 2, axis=-1)
    x_c = lax.conv_general_dilated(x_m, conv_w[:, None, :], window_strides=(1,),
                                   padding=[(CONV_WIDTH - 1, 0)],
                                   dimension_numbers=('NWC', 'WIO', 'NWC'),
                                   feature_group_count=INNER_C)
    x_c = jax.nn.silu(x_c + conv_b)
    blockdiag = lambda t, w: jnp.einsum('bsgi,gio->bsgo', t.reshape(b, s, -1, QKV_BLOCK), w).reshape(b, s, INNER_C)
    q, k, v = blockdiag(x_c, wq), blockdiag(x_c, wk), blockdiag(x_m, wv)
    gates = (jnp.concatenate([q, k, v], axis=-1) @ w_gates + b_gates).astype(jnp.float32)
    ig = gates[..., :N_HEADS_C].transpose(0, 2, 1)
    fg = gates[..., N_HEADS_C:].transpose(0, 2, 1)
    heads = lambda t: t.reshape(b, s, N_HEADS_C, HEAD_DIM_C).transpose(0, 2, 1, 3).astype(jnp.float32)
    hh = mlstm_chunkwise(heads(q), heads(k) * HEAD_DIM_C ** -0.5, heads(v), ig, fg)
    hh = rms_norm(hh.transpose(0, 2, 1, 3), out_gain.reshape(N_HEADS_C, HEAD_DIM_C))
    hh = hh.reshape(b, s, INNER_C).astype(xn.dtype)
    y = (hh + skip * x_c) * jax.nn.silu(z)
    return y @ w_out

def setup_inputs(seed: int = 0) -> dict:
    key = jax.random.key(seed)
    ks = iter(jax.random.split(key, 40))
    nrm = lambda shape, fan_in: jax.random.normal(next(ks), shape, jnp.float32) * fan_in ** -0.5
    gain = lambda shape: 1.0 + 0.02 * jax.random.normal(next(ks), shape, jnp.float32)
    x = jax.random.normal(next(ks), (BATCH, SEQ, D_MODEL), jnp.float32)
    rel_bias = 0.5 * jax.random.normal(next(ks), (REL_BUCKETS, N_HEADS_A), jnp.float32)
    norm_gains = gain((DEPTH, 3, D_MODEL))
    ffn_w_gate = nrm((DEPTH, 2, D_MODEL, D_FF), D_MODEL)
    ffn_w_up = nrm((DEPTH, 2, D_MODEL, D_FF), D_MODEL)
    ffn_w_down = nrm((DEPTH, 2, D_FF, D_MODEL), D_FF)
    ev_w_in = nrm((N_EVEN, D_MODEL, IN_WIDTH_EVEN), D_MODEL)
    ev_q_gain = gain((N_EVEN, HEAD_DIM_A))
    ev_k_gain = gain((N_EVEN, HEAD_DIM_A))
    ev_pool_w = nrm((N_EVEN, N_POOL_GROUPS, POOL_GROUP_DIM, POOL_GROUP_DIM), POOL_GROUP_DIM)
    ev_pool_scale = gain((N_EVEN, WIDTH_B))
    ev_w_out = nrm((N_EVEN, MIX_WIDTH_EVEN, D_MODEL), MIX_WIDTH_EVEN)
    od_w_in = nrm((N_ODD, D_MODEL, 2 * INNER_C), D_MODEL)
    od_conv_w = nrm((N_ODD, CONV_WIDTH, INNER_C), CONV_WIDTH)
    od_conv_b = 0.02 * jax.random.normal(next(ks), (N_ODD, INNER_C), jnp.float32)
    od_wq = nrm((N_ODD, INNER_C // QKV_BLOCK, QKV_BLOCK, QKV_BLOCK), QKV_BLOCK)
    od_wk = nrm((N_ODD, INNER_C // QKV_BLOCK, QKV_BLOCK, QKV_BLOCK), QKV_BLOCK)
    od_wv = nrm((N_ODD, INNER_C // QKV_BLOCK, QKV_BLOCK, QKV_BLOCK), QKV_BLOCK)
    od_w_gates = nrm((N_ODD, 3 * INNER_C, 2 * N_HEADS_C), 3 * INNER_C)
    od_b_gates = jnp.concatenate([
        0.1 * jax.random.normal(next(ks), (N_ODD, N_HEADS_C), jnp.float32),
        jax.random.uniform(next(ks), (N_ODD, N_HEADS_C), jnp.float32, 3.0, 6.0)],
        axis=-1)
    od_skip = gain((N_ODD, INNER_C))
    od_out_gain = gain((N_ODD, INNER_C))
    od_w_out = nrm((N_ODD, INNER_C, D_MODEL), INNER_C)
    return {'x': x, 'rel_bias': rel_bias, 'norm_gains': norm_gains,
            'ffn_w_gate': ffn_w_gate, 'ffn_w_up': ffn_w_up, 'ffn_w_down': ffn_w_down,
            'ev_w_in': ev_w_in, 'ev_q_gain': ev_q_gain, 'ev_k_gain': ev_k_gain,
            'ev_pool_w': ev_pool_w, 'ev_pool_scale': ev_pool_scale, 'ev_w_out': ev_w_out,
            'od_w_in': od_w_in, 'od_conv_w': od_conv_w, 'od_conv_b': od_conv_b,
            'od_wq': od_wq, 'od_wk': od_wk, 'od_wv': od_wv,
            'od_w_gates': od_w_gates, 'od_b_gates': od_b_gates, 'od_skip': od_skip,
            'od_out_gain': od_out_gain, 'od_w_out': od_w_out}

def reference(x, rel_bias, norm_gains, ffn_w_gate, ffn_w_up, ffn_w_down,
              ev_w_in, ev_q_gain, ev_k_gain, ev_pool_w, ev_pool_scale, ev_w_out,
              od_w_in, od_conv_w, od_conv_b, od_wq, od_wk, od_wv,
              od_w_gates, od_b_gates, od_skip, od_out_gain, od_w_out):
    for layer in range(DEPTH):
        g = norm_gains[layer]
        x = x + FFN_RESIDUAL * swiglu(rms_norm(x, g[0]), ffn_w_gate[layer, 0],
                                      ffn_w_up[layer, 0], ffn_w_down[layer, 0])
        xn = rms_norm(x, g[1])
        if layer % 2 == 0:
            i = layer // 2
            x = x + dilated_pool_mixer(xn, rel_bias, ev_w_in[i], ev_q_gain[i], ev_k_gain[i],
                                       ev_pool_w[i], ev_pool_scale[i], ev_w_out[i])
        else:
            i = layer // 2
            x = x + mlstm_mixer(xn, od_w_in[i], od_conv_w[i], od_conv_b[i], od_wq[i], od_wk[i],
                                od_wv[i], od_w_gates[i], od_b_gates[i], od_skip[i],
                                od_out_gain[i], od_w_out[i])
        x = x + FFN_RESIDUAL * swiglu(rms_norm(x, g[2]), ffn_w_gate[layer, 1],
                                      ffn_w_up[layer, 1], ffn_w_down[layer, 1])
    return x


_drawn_inputs = setup_inputs


def setup_inputs(seed=0):
    import zlib

    import numpy as np

    out = dict(_drawn_inputs(seed))
    spreads = {}
    factors = {'ev_q_gain': 8.0,
     'ev_k_gain': 8.0,
     'ev_pool_scale': 3.822,
     'od_conv_b': 4.282,
     'od_skip': 8.0,
     'od_out_gain': 6.877}
    for name, (base, spread) in spreads.items():
        noise = np.random.default_rng([zlib.crc32(name.encode()), seed]).standard_normal(out[name].shape)
        drawn = base * np.exp(spread * noise) if base else spread * noise
        out[name] = __import__('jax').numpy.asarray(drawn.astype(out[name].dtype))
    for name, factor in factors.items():
        out[name] = (out[name] * factor).astype(out[name].dtype)
    return out
```

```python
import math
from contextlib import ExitStack

import numpy as np

import concourse.bass as bass
from concourse import mybir

F32 = mybir.dt.float32
F32R = mybir.dt.float32r
ACT = mybir.ActivationFunctionType
ALU = mybir.AluOpType

P = 128
T = 512
DM = 1024
KX = DM // P
NFFN = 4
FF = 2816
FT = FF // P
SLOTS = 4
KMAX = 8
EPS = 1e-6

HA, EA = 8, 64
NG = 4
WINDOWS = (2, 4, 8, 16)
PAD = 16
PATTERNS = ((128, 1), (512, 4), (2048, 16))
BUCKETS, MAX_DISTANCE = 32, 2048
BW = T + P
NEG = -1e30

HC = 4
INNER = 2 * DM
CT = INNER // P
HT_ = CT // HC
EC = INNER // HC
TAPS = 4
TT = T // P

FFN_QUADS = 17
Q_FFN = (0, 23, 40, 69)
Q_EIN, Q_EOUT = 17, 21
Q_OIN, Q_OOUT = 57, 65
Q_END = 86

C_NORM, C_CONV, C_CONVB, C_SKIP, C_GAIN, C_PSC, C_QG, C_KG, C_BG = 0, 48, 112, 128, 144, 160, 164, 165, 166
NPAR = 167
K_ID, K_ONE, K_HS, K_MASK, K_FIX = 0, 128, 256, 384, 416
NCST = 480


def t5_bucket(d):
    exact = BUCKETS // 2
    f = np.maximum(d.astype(np.float32), np.float32(1))
    large = exact + (np.log(f / exact) / np.float32(math.log(MAX_DISTANCE / exact)) * (BUCKETS - exact)).astype(np.int32)
    return np.where(d < exact, d, np.minimum(large, BUCKETS - 1))


def shape_constants():
    c = np.zeros((P, NCST), np.float32)
    c[:, K_ID:K_ID + P] = np.eye(P)
    c[:, K_ONE:K_ONE + P] = 1
    for m in range(8):
        for half in range(2):
            c[64 * half:64 * half + 64, K_HS + 16 * m + 2 * m + half] = 1
    for g in range(32):
        c[4 * g:4 * g + 4, K_MASK + g] = 1
    for g, w in enumerate(WINDOWS):
        c[:, K_FIX + 16 * g:K_FIX + 16 * g + 16] = w / np.minimum(np.arange(1, 17), w)
    d = T - 1 - np.arange(BW)
    hot = np.zeros((BUCKETS + 1, BW), np.float32)
    count = np.zeros(BW)
    for window, dilation in PATTERNS:
        count += (d >= 0) & (d <= window) & (d % dilation == 0)
    b = t5_bucket(np.maximum(d, 0))
    for z in range(BW):
        if count[z]:
            hot[b[z], z] = 1
            hot[BUCKETS, z] = math.log(count[z])
        else:
            hot[BUCKETS, z] = NEG
    pick = np.concatenate([c[:, K_HS + 16 * m:K_HS + 16 * m + 16].T for m in range(8)], 1)
    return c, hot, pick


def core_items():
    items = []
    for h in range(HC):
        items += [(h, "q", c) for c in range(HT_)] + [(h, "k", c) for c in range(HT_)]
        if h:
            items.append((h - 1, "ms", 0))
        items += [(h, "v", c) for c in range(HT_)] + [(h, "M", 0), (h, "EM", 0)]
        items += [(h, "s", j) for j in range(TT)]
    items.append((HC - 1, "ms", 0))
    return {item: r for r, item in enumerate(items)}


def trunk(nc, xT, par_d, cst_d, hot_d, relb_d, w3_d, wgr_d, poolw_d, pick_d, gu_d, down_d, down2_d, ein_d, eout_d, oin_d,
          oout_d, skew_d, out_d):
    ctx = ExitStack()
    with ctx:
        def sb(name, shape, dt=F32):
            return ctx.enter_context(nc.sbuf_tensor(name, shape, dt))

        def sem(name):
            return ctx.enter_context(nc.semaphore(name))

        X = sb("X", [P, KX, T])
        RSTD = sb("RSTD", [P, T])
        SQ = sb("SQ", [P, T])
        TMP = sb("TMP", [P, 8, T])
        PAR = sb("PAR", [P, NPAR])
        CST = sb("CST", [P, NCST])
        W3 = sb("W3", [P, 3, CT, 4])
        WP = sb("WP", [P, 2 * CT, 2 * HC])
        EPST = sb("EPST", [P, 1])
        QG = sb("QG", [P, 1])
        ATT = sb("ATT", [P, 3, 4 * HA])
        ACOL = sb("ACOL", [P, TT, HC])

        def region(name, nbytes):
            base = nc.sbuf_base
            sb(name, [P, nbytes // 4])
            return base

        TB = T * 4
        ring0 = region("ring", 2 * SLOTS * KMAX * P * 4)
        xr0 = region("x_region", 16 * TB)
        hr0 = region("h_region", 16 * TB)
        e0 = region("mixer_region", 34 * TB)

        def at(name, shape, base, offset, dt=F32):
            return nc.alloc_sbuf_tensor_at(name, shape, dt, offset=base + offset)

        SB = KMAX * P * 4
        RAW = [at(f"RAW{s}", [P, KMAX * P], ring0, 2 * s * SB) for s in range(SLOTS)]
        LO = [at(f"LO{s}", [P, KMAX * P], ring0, 2 * s * SB, F32R) for s in range(SLOTS)]
        HI = [at(f"HI{s}", [P, KMAX * P], ring0, (2 * s + 1) * SB, F32R) for s in range(SLOTS)]
        XH = at("XH", [P, KX, T], xr0, 0, F32R)
        XL = at("XL", [P, KX, T], xr0, 8 * TB, F32R)
        HH = at("HH", [P, 8, T], hr0, 0, F32R)
        HL = at("HL", [P, 8, T], hr0, 8 * TB, F32R)
        STG = at("STG", [P, HA, BW], e0, 0)
        RELB = at("RELB", [BUCKETS + 1, HA], e0, 20480)
        HOT = at("HOT", [BUCKETS + 1, BW], e0, 20544)
        QK = at("QK", [P, 8, T], e0, 0)
        SQB = at("SQB", [P, 8, T], e0, 8 * TB)
        V = SQB
        G = at("G", [P, HA, T], e0, 16 * TB)
        U = at("U", [P, NG, PAD + T], e0, 24 * TB)
        WSUM = at("WSUM", [P, 2, PAD + T], e0, 24 * TB + NG * (PAD + T) * 4)
        POOLW = at("POOLW", [P, NG, P], e0, 31 * TB)
        PICK = at("PICK", [16, 8 * P], e0, 32 * TB)
        WGR = at("WGR", [P, 3, CT, 4, 2 * HC], e0, 29 * TB)
        XM = at("XM", [P, CT, T], e0, 0)
        XC = at("XC", [P, CT, T], e0, CT * TB)
        MROW = at("MROW", [HC, T], e0, 2 * CT * TB)
        EMROW = at("EMROW", [HC, T], e0, (2 * CT + 1) * TB)
        YH = at("YH", [P, CT, T], e0, 0, F32R)
        YL = at("YL", [P, CT, T], e0, CT * TB, F32R)
        SZ = at("SZ", [P, CT, T], hr0, 0)
        Q = at("Q", [P, HT_, T], xr0, 0)
        K = at("K", [P, HT_, T], xr0, 4 * TB)
        PT = at("PT", [P, TT, T], xr0, 8 * TB)
        BD = at("BD", [P, 3, HT_, P], xr0, 12 * TB)
        SQX = at("SQX", [P, T], xr0, 15 * TB)

        GT, SG, SR, HT = (TMP[:, 2 * i:2 * i + 2, :] for i in range(4))

        ident = CST[:, K_ID:K_ID + P]
        ones = CST[:, K_ONE:K_ONE + P]

        def par(col):
            return PAR[:, col:col + 1]

        PS = [ctx.enter_context(nc.psum_tensor(f"PS{b}", [P, T], F32)) for b in range(8)]
        AUX = PS[4]

        par_in, x_in, hot_in, skew_out, skew_in, prep_in, out_done = (
            sem(n) for n in ("par_in", "x_in", "hot_in", "skew_out", "skew_in", "prep_in", "out_done"))
        weights_in = [sem(f"weights_in{s}") for s in range(SLOTS)]
        hi_ready, lo_ready, unit_done = sem("hi_ready"), sem("lo_ready"), sem("unit_done")
        bank_free = sem("bank_free")
        silu_ready, sr_ready, hh_ready, hl_ready = (sem(n) for n in ("silu_ready", "sr_ready", "hh_ready", "hl_ready"))
        xh_ready, xl_ready, sqt_ready, sq_ready = (sem(n) for n in ("xh_ready", "xl_ready", "sqt_ready", "sq_ready"))
        norm_sum, std_ready, rstd_ready = sem("norm_sum"), sem("std_ready"), sem("rstd_ready")
        small_ready = sem("small_ready")
        bias_sum, bias_staged = sem("bias_sum"), sem("bias_staged")
        qk_sq, qk_rows, row_std, row_rstd, qk_bcast, qk_normed = (
            sem(n) for n in ("qk_sq", "qk_rows", "row_std", "row_rstd", "qk_bcast", "qk_normed"))
        v_turned, v_ready = sem("v_turned"), sem("v_ready")
        s_done, s_shift, p_exp, p_inv, p_ready, pt_done, pt_ready, pv_done = (
            sem(n) for n in ("s_done", "s_shift", "p_exp", "p_inv", "p_ready", "pt_done", "pt_ready", "pv_done"))
        attn_hi, attn_lo, diff_ready, pool_mm, pool_hi, pool_lo = (
            sem(n) for n in ("attn_hi", "attn_lo", "diff_ready", "pool_mm", "pool_hi", "pool_lo"))
        tap0, conv_step, xc_ready, sz_ready, prep_ready = (
            sem(n) for n in ("tap0", "conv_step", "xc_ready", "sz_ready", "prep_ready"))
        gate_sum, gate_rows, fg_rows, fg_abs, log_rows, a_rows, m_rows, em_rows, a_turned, acol_ready = (
            sem(n) for n in ("gate_sum", "gate_rows", "fg_rows", "fg_abs", "log_rows", "a_rows", "m_rows", "em_rows", "a_turned",
                             "acol_ready"))
        bd_ready, item_done = sem("bd_ready"), sem("item_done")
        item_read = [sem(f"item_read{b}") for b in range(3)]
        wt_exp, wt_ready = sem("wt_exp"), sem("wt_ready")
        num_done, den_abs, num_sq, ssq_step, tstd_ready, num_read = (
            sem(n) for n in ("num_done", "den_abs", "num_sq", "ssq_step", "tstd_ready", "num_read"))
        y_pre, y_ready, yh_ready, yl_ready = (sem(n) for n in ("y_pre", "y_ready", "yh_ready", "yl_ready"))
        vector_step, scalar_step, pool_step = sem("vector_step"), sem("scalar_step"), sem("pool_step")

        ITEM = core_items()
        ROWS = [(hp, i, half) for hp in range(HA // 2) for i in range(TT) for half in range(2)]
        POOL_AT = {8 + 5 * g: g for g in range(NG)}

        def read_out(eng, item):
            r = ITEM[item]
            eng.wait_ge(item_read[r % 3], r // 3 + 1)

        def read_through(eng, item):
            for r in range(ITEM[item] - 2, ITEM[item] + 1):
                eng.wait_ge(item_read[r % 3], r // 3 + 1)

        def walk_ffn(eng, step):
            with eng.Fori(0, 2) as third:
                for lq in range(6):
                    step(third, lq, False)
            for lq in range(5):
                step(2, lq, True)

        def is_gate_up(lq, last):
            return lq < (3 if last else 4)

        block = ctx.enter_context(nc.Block())

        @block.sync
        def _(sp):
            def load(q, j, src):
                sp.wait_ge(unit_done, 4 * q + j - 3)
                sp.dma_start(RAW[j][:, 0:src.shape[1]], src).then_inc(weights_in[j], 16)

            def ffn(f, q0, after):
                def step(third, lq, last):
                    q = q0 + 6 * third + lq + 1
                    for j in range(SLOTS):
                        if last and lq == 4:
                            if after is not None:
                                load(q, j, after[j])
                        elif last:
                            load(q, j, gu_d[f, 32 + 4 * (lq + 1) + j] if lq + 1 < 3
                                 else down2_d[f, 4 * (lq - 2) + j])
                        elif lq + 1 < 4:
                            load(q, j, gu_d[f, third * 16 + (4 * (lq + 1) + j)])
                        elif lq + 1 < 6:
                            load(q, j, down_d[f, third * 8 + (4 * (lq - 3) + j)])
                        else:
                            load(q, j, gu_d[f, third * 16 + (16 + j)])
                walk_ffn(sp, step)

            def projection(q0, n, src, after):
                with sp.Fori(1, n) as i:
                    for j in range(SLOTS):
                        load(q0 + i, j, src[i * 4 + j])
                for j in range(SLOTS):
                    load(q0 + n, j, after[j])

            sp.dma_start(PAR[:], par_d).then_inc(par_in, 16)
            sp.dma_start(CST[:], cst_d).then_inc(par_in, 16)
            sp.dma_start(RELB[:], relb_d).then_inc(hot_in, 16)
            sp.dma_start(HOT[:], hot_d).then_inc(hot_in, 16)
            sp.dma_start(X[:], xT).then_inc(x_in, 16)
            for j in range(SLOTS):
                sp.dma_start(RAW[j][:], gu_d[0, j]).then_inc(weights_in[j], 16)
            sp.wait_ge(bias_staged, 2 * HA)
            sp.dma_start(skew_d.rearrange("h p z -> p h z"), STG[:]).then_inc(skew_out, 16)
            sp.wait_ge(skew_out, 16)
            for h in range(HA):
                flat = skew_d[h].rearrange("p z -> (p z)")
                skewed = flat[P - 1:P - 1 + P * (BW - 1)].rearrange("(p z) -> p z", z=BW - 1)[:, 0:T]
                sp.dma_start(G[:, h, :], skewed).then_inc(skew_in, 16)
            sp.dma_start(POOLW[:], poolw_d).then_inc(prep_in, 16)
            sp.dma_start(PICK[:], pick_d).then_inc(prep_in, 16)
            sp.dma_start(W3[:], w3_d).then_inc(prep_in, 16)

            ffn(0, Q_FFN[0], ein_d)
            projection(Q_EIN, 4, ein_d, eout_d)
            projection(Q_EOUT, 2, eout_d, gu_d[1])
            ffn(1, Q_FFN[1], gu_d[2])
            sp.dma_start(WGR[:].rearrange("p a c o n -> p (a c o n)"), wgr_d).then_inc(prep_in, 16)
            ffn(2, Q_FFN[2], oin_d)
            projection(Q_OIN, 8, oin_d, oout_d)
            projection(Q_OOUT, 4, oout_d, gu_d[3])
            ffn(3, Q_FFN[3], None)
            for m in range(KX):
                sp.wait_ge(bank_free, 4 * Q_END - 8 + m + 5)
                sp.dma_start(out_d[:, m, :], X[:, m, :]).then_inc(out_done, 16)
            sp.wait_ge(out_done, 16 * KX)

        @block.tensor
        def _(pe):
            def unit(q, j, kt, hi, lo, order=None, ready=None):
                pe.wait_ge(lo_ready, 4 * q + j + 1)
                pe.wait_ge(bank_free, 4 * q + j + 1)
                order = order or list(range(kt))
                for n, k in enumerate(order):
                    if ready:
                        ready(k)
                    c = slice(k * P, k * P + P)
                    pe.matmul(PS[j][:], HI[j][:, c], hi(k), start=(n == 0), stop=False)
                    pe.matmul(PS[j][:], HI[j][:, c], lo(k), start=False, stop=False)
                    last = pe.matmul(PS[j][:], LO[j][:, c], hi(k), start=False, stop=(n == kt - 1))
                last.then_inc(unit_done, 1)

            def xh(k):
                return XH[:, k, :]

            def xl(k):
                return XL[:, k, :]

            def x_tile_ready(r):
                return lambda k: pe.wait_ge(xl_ready, 8 * r + k + 1)

            def norm(r):
                pe.wait_ge(sq_ready, 8 * r + 8)
                pe.matmul(AUX[:], ones, SQ[:], start=True, stop=True).then_inc(norm_sum, 1)

            def ffn(f, q0, r):
                unit(q0, 0, KX, xh, xl, ready=x_tile_ready(r))
                norm(r)

                def quad(q, third, lq, last, first=0):
                    for j in range(first, SLOTS):
                        if is_gate_up(lq, last):
                            unit(q, j, KX, xh, xl)
                        else:
                            kt = 6 if last else 8
                            pair = 22 * f + 8 * third
                            tile_ready = (lambda k: pe.wait_ge(hl_ready, pair + (k + 1))) if j == 0 else None
                            unit(q, j, kt, lambda k: HH[:, k, :], lambda k: HL[:, k, :], ready=tile_ready)

                quad(q0, 0, 0, False, first=1)
                for lq in range(1, 6):
                    quad(q0 + lq, 0, lq, False)
                for lq in range(6):
                    quad(q0 + 6 + lq, 1, lq, False)
                for lq in range(5):
                    quad(q0 + 12 + lq, 2, lq, True)

            def even_mixer():
                q0 = Q_EIN
                unit(q0, 0, KX, xh, xl, ready=x_tile_ready(1))
                norm(1)
                for j in range(1, SLOTS):
                    unit(q0, j, KX, xh, xl)
                with pe.Fori(1, 3) as i:
                    for j in range(SLOTS):
                        unit(q0 + i, j, KX, xh, xl)
                for m in range(8):
                    pe.wait_ge(qk_sq, m + 1)
                    last = pe.matmul(PS[5][0:16, :], CST[:, K_HS + 16 * m:K_HS + 16 * m + 16], SQB[:, m, :],
                                     start=(m == 0), stop=(m == 7))
                last.then_inc(qk_rows, 1)
                for j in range(SLOTS):
                    unit(q0 + 3, j, KX, xh, xl)
                for m in range(4):
                    if m >= 2:
                        pe.wait_ge(v_ready, m - 1)
                    pe.wait_ge(bank_free, 4 * (q0 + 2) + m + 5)
                    for j in range(TT):
                        last = pe.transpose(PS[6 + m % 2][:, j * P:j * P + P], TMP[:, m, j * P:j * P + P], ident)
                    last.then_inc(v_turned, 1)
                pe.wait_ge(row_rstd, 1)
                pe.wait_ge(prep_in, 48)
                for n, m in enumerate((0, 4, 1, 5, 2, 6, 3, 7)):
                    if n >= 2:
                        pe.wait_ge(qk_normed, n - 1)
                    pe.matmul(PS[4 + n % 2][:], PICK[:, m * P:m * P + P], RSTD[0:16, :], start=True, stop=True).then_inc(qk_bcast, 1)

                pe.wait_ge(bank_free, 4 * Q_EOUT + 4)

                def scores(a):
                    hp, i, half = ROWS[a]
                    n = (i + 1) * P
                    h = slice(64 * half, 64 * half + 64)
                    if i == 0 and half == 0:
                        pe.wait_ge(qk_normed, 2 * hp + 2)
                    if a >= 2:
                        pe.wait_ge(s_shift, a - 1)
                    pe.matmul(PS[a % 2][:, 0:n], QK[h, hp, i * P:i * P + P], QK[h, 4 + hp, 0:n],
                              start=True, stop=True).then_inc(s_done, 1)

                def turn(a):
                    _, i, _ = ROWS[a]
                    pe.wait_ge(p_ready, a + 1)
                    if a >= 2:
                        pe.wait_ge(pt_ready, a - 1)
                    for j in range(i + 1):
                        last = pe.transpose(PS[2 + a % 2][:, j * P:j * P + P], TMP[:, 2 + a % 3, j * P:j * P + P],
                                            ident)
                    last.then_inc(pt_done, 1)

                def values(a):
                    hp, i, half = ROWS[a]
                    head = 2 * hp + half
                    pe.wait_ge(pt_ready, a + 1)
                    if a == 0:
                        pe.wait_ge(v_ready, 4)
                    if i == 0 and half == 0 and hp >= 2:
                        pe.wait_ge(attn_lo, hp - 1)
                    for j in range(i + 1):
                        last = pe.matmul(PS[6 + hp % 2][64 * half:64 * half + 64, i * P:i * P + P],
                                         V[:, j, EA * head:EA * head + EA], TMP[:, 5 + a % 3, j * P:j * P + P],
                                         start=(j == 0), stop=(j == i))
                    last.then_inc(pv_done, 1)

                def pool_group(g):
                    pe.wait_ge(diff_ready, g + 1)
                    if g == 0:
                        pe.wait_ge(qk_normed, 8)
                    if g >= 2:
                        pe.wait_ge(pool_lo, g - 1)
                    pe.matmul(PS[4 + g % 2][:], POOLW[:, g, :], U[:, g, PAD:], start=True,
                              stop=True).then_inc(pool_mm, 1)

                for a in range(len(ROWS) + 3):
                    if a < len(ROWS):
                        scores(a)
                    if a in POOL_AT:
                        pool_group(POOL_AT[a])
                    if 2 <= a < len(ROWS) + 2:
                        turn(a - 2)
                    if a >= 3:
                        values(a - 3)

                def mixed_ready(k):
                    pe.wait_ge(pool_lo if k >= 4 else attn_lo, k % 4 + 1)

                for q in range(2):
                    for j in range(SLOTS):
                        unit(Q_EOUT + q, j, KX, lambda k: HH[:, k, :], lambda k: HL[:, k, :],
                             order=[4, 5, 6, 7, 0, 1, 2, 3], ready=mixed_ready if q == 0 and j == 0 else None)

            def odd_mixer():
                q0 = Q_OIN
                unit(q0, 0, KX, xh, xl, ready=x_tile_ready(4))
                norm(4)
                for j in range(1, SLOTS):
                    unit(q0, j, KX, xh, xl)
                with pe.Fori(1, 8) as i:
                    for j in range(SLOTS):
                        unit(q0 + i, j, KX, xh, xl)
                pe.wait_ge(prep_ready, 2)
                pe.wait_ge(xc_ready, CT)
                for n in range(2 * CT):
                    src = XC[:, n, :] if n < CT else XM[:, n - CT, :]
                    last = pe.matmul(AUX[0:8, :], WP[:, n, :], src, start=(n == 0), stop=(n == 2 * CT - 1))
                last.then_inc(gate_sum, 1)

                def bank(item):
                    r = ITEM[item]
                    if r >= 3:
                        pe.wait_ge(item_read[r % 3], r // 3)
                    return PS[5 + r % 3]

                def projected(h, name, t):
                    for c in range(HT_):
                        ps = bank((h, name, c))
                        pe.matmul(ps[:], BD[:, t, c, :], XC[:, HT_ * h + c, :], start=True,
                                  stop=True).then_inc(item_done, 1)

                def mean_square(h):
                    ps = bank((h, "ms", 0))
                    pe.wait_ge(ssq_step, 3 * h + 3)
                    pe.matmul(ps[:], ones, SQ[:], start=True, stop=True).then_inc(item_done, 1)

                for h in range(HC):
                    pe.wait_ge(bd_ready, h + 1)
                    projected(h, "q", 0)
                    if h == 0:
                        pe.wait_ge(gate_rows, 1)
                        pe.wait_ge(bank_free, 4 * Q_OOUT + 4)
                        pe.matmul(PS[0][0:HC, :], ident[0:8, HC:2 * HC], TMP[0:8, 0, :], start=True,
                                  stop=True).then_inc(fg_rows, 1)
                    projected(h, "k", 1)
                    if h:
                        mean_square(h - 1)
                    for c in range(HT_):
                        ps = bank((h, "v", c))
                        for j in range(TT):
                            last = pe.matmul(ps[:, j * P:j * P + P], XM[:, HT_ * h + c, j * P:j * P + P],
                                             BD[:, 2, c, :], start=True, stop=True)
                        last.then_inc(item_done, 1)
                    if h == 0:
                        pe.wait_ge(a_rows, 1)
                        for j in range(TT):
                            last = pe.transpose(PS[1][:, HC * j:HC * j + HC], TMP[0:HC, 6, j * P:j * P + P],
                                                ident[0:HC, 0:HC])
                        last.then_inc(a_turned, 1)
                        pe.wait_ge(m_rows, 1)
                        pe.wait_ge(em_rows, 1)
                    pick = ident[0:HC, h:h + 1].to_broadcast([HC, P])
                    ps = bank((h, "M", 0))
                    pe.matmul(ps[:], pick, MROW[:], start=True, stop=True).then_inc(item_done, 1)
                    ps = bank((h, "EM", 0))
                    pe.matmul(ps[:], pick, EMROW[:], start=True, stop=True).then_inc(item_done, 1)
                    read_through(pe, (h, "k", HT_ - 1))
                    for j in range(TT):
                        ps = bank((h, "s", j))
                        for c in range(HT_):
                            last = pe.matmul(ps[:, 0:T - P * j], K[:, c, j * P:j * P + P], Q[:, c, j * P:],
                                             start=(c == 0), stop=(c == HT_ - 1))
                        last.then_inc(item_done, 1)
                    if h:
                        pe.wait_ge(num_read, HT_ * h)
                    else:
                        pe.wait_ge(acol_ready, 1)
                        pe.wait_ge(em_rows, 1)
                    for j in range(TT):
                        read_out(pe, (h, "s", j))
                        for c in range(HT_):
                            last = pe.matmul(PS[c][:, j * P:], XM[:, HT_ * h + c, j * P:j * P + P],
                                             PT[:, j, 0:T - P * j], start=(j == 0), stop=(j == TT - 1))
                        last = pe.matmul(PS[4][:, j * P:], ones, PT[:, j, 0:T - P * j], start=(j == 0),
                                         stop=(j == TT - 1))
                    last.then_inc(num_done, 1)
                mean_square(HC - 1)

                def y_tile_ready(half):
                    return lambda k: pe.wait_ge(yl_ready, 8 * half + k + 1)

                for half in range(2):
                    for q in range(2):
                        for j in range(SLOTS):
                            if half == 0 and q == 0 and j == 0:
                                pe.wait_ge(num_read, CT)
                            unit(Q_OOUT + 2 * half + q, j, KX, lambda k: YH[:, 8 * half + k, :],
                                 lambda k: YL[:, 8 * half + k, :],
                                 ready=y_tile_ready(half) if q == 0 and j == 0 else None)

            pe.wait_ge(par_in, 32)
            pe.wait_ge(hot_in, 32)
            for h in range(HA):
                pick = RELB[:, h:h + 1].to_broadcast([BUCKETS + 1, P])
                for part, (z0, z1) in enumerate(((0, T), (T, BW))):
                    n = 2 * h + part
                    if n >= 2:
                        pe.wait_ge(bias_staged, n - 1)
                    pe.matmul(PS[6 + n % 2][:, 0:z1 - z0], pick, HOT[:, z0:z1], start=True,
                              stop=True).then_inc(bias_sum, 1)
            ffn(0, Q_FFN[0], 0)
            even_mixer()
            ffn(1, Q_FFN[1], 2)
            ffn(2, Q_FFN[2], 3)
            odd_mixer()
            ffn(3, Q_FFN[3], 5)

        @block.scalar
        def _(act):
            steps = [0]

            def link(ins):
                steps[0] += 1
                ins.then_inc(scalar_step, 1)
                act.wait_ge(scalar_step, steps[0])

            def split_hi(q, j, kt):
                act.wait_ge(weights_in[j], 16 * (q + 1))
                act.activation(HI[j][:, 0:kt * P], RAW[j][:, 0:kt * P], ACT.Copy).then_inc(hi_ready, 1)

            def new_x_tile(r, m):
                act.activation(XH[:, m, :], X[:, m, :], ACT.Copy, scale=par(C_NORM + 8 * r + m)).then_inc(xh_ready, 1)
                if 8 * r + m >= 2:
                    act.wait_ge(sq_ready, 8 * r + m - 1)
                act.activation(GT[:, m % 2, :], X[:, m, :], ACT.Square).then_inc(sqt_ready, 1)

            def norm(r):
                act.wait_ge(norm_sum, r + 1)
                act.activation(RSTD[:], AUX[:], ACT.Sqrt, scale=1.0 / DM, bias=EPST[:]).then_inc(std_ready, 1)

            def residual_tile(q, j, r, m):
                if r is not None:
                    act.wait_ge(bank_free, 4 * q + j + 5)
                    new_x_tile(r, m)

            def ffn(f, q0, r, after):
                def step(third, lq, last):
                    q = q0 + 6 * third + lq
                    for j in range(SLOTS):
                        if is_gate_up(lq, last):
                            m = 2 * lq + j // 2
                            act.wait_ge(bank_free, 4 * q + j + 5)
                            if j % 2 == 0:
                                act.activation(SG[:, m % 2, :], GT[:, m % 2, :], ACT.Silu).then_inc(silu_ready, 1)
                            else:
                                act.activation(HH[:, m, :], HT[:, m % 2, :], ACT.Copy).then_inc(hh_ready, 1)
                        elif last and after:
                            residual_tile(q, j, r, 4 * (lq - 3) + j)
                        if last and lq >= 2:
                            if lq < 4:
                                split_hi(q + 1, j, 6)
                            elif after:
                                split_hi(q + 1, j, 8)
                        else:
                            split_hi(q + 1, j, 8)
                walk_ffn(act, step)

            def even_mixer():
                for lq in range(4):
                    for j in range(SLOTS):
                        u = 4 * lq + j
                        if u < 8:
                            act.wait_ge(bank_free, 4 * (Q_EIN + lq) + j + 5)
                            act.activation(SQB[:, u, :], QK[:, u, :], ACT.Square).then_inc(qk_sq, 1)
                        split_hi(Q_EIN + lq + 1, j, 8)
                act.wait_ge(qk_rows, 1)
                act.wait_ge(bank_free, 4 * Q_EOUT + 4)
                act.activation(RSTD[0:16, :], PS[5][0:16, :], ACT.Sqrt, scale=1.0 / EA,
                               bias=EPST[0:16, :]).then_inc(row_std, 1)
                for m in range(4):
                    act.wait_ge(v_turned, m + 1)
                    act.activation(V[:, 0:4, m * P:m * P + P],
                                   PS[6 + m % 2][:].rearrange("p (j f) -> p j f", j=TT), ACT.Copy).then_inc(v_ready, 1)

                def exponentials(a):
                    _, i, _ = ROWS[a]
                    n = (i + 1) * P
                    act.wait_ge(s_shift, a + 1)
                    if a >= 3:
                        act.wait_ge(pt_done, a - 2)
                    act.activation(TMP[:, 2 + a % 3, 0:n], TMP[:, a % 2, 0:n], ACT.Exp, scale=-1.0,
                                   bias=ATT[:, 0, a:a + 1], accum_out=ATT[:, 1, a:a + 1]).then_inc(p_exp, 1)

                def turned(a):
                    _, i, _ = ROWS[a]
                    n = (i + 1) * P
                    act.wait_ge(pt_done, a + 1)
                    if a >= 3:
                        act.wait_ge(pv_done, a - 2)
                    act.activation(TMP[:, 5 + a % 3, 0:n], PS[2 + a % 2][:, 0:n], ACT.Copy).then_inc(pt_ready, 1)

                for a in range(len(ROWS) + 5):
                    if a < len(ROWS):
                        exponentials(a)
                    if 2 <= a < len(ROWS) + 2:
                        turned(a - 2)
                    if a - 2 in POOL_AT:
                        g = POOL_AT[a - 2]
                        act.wait_ge(pool_mm, g + 1)
                        act.activation(HH[:, 4 + g, :], PS[4 + g % 2][:], ACT.Copy,
                                       scale=par(C_PSC + g)).then_inc(pool_hi, 1)
                    if a >= 12 and (a - 12) % 8 == 0:
                        hp = (a - 12) // 8
                        act.wait_ge(pv_done, 8 * hp + 8)
                        act.activation(HH[:, hp, :], PS[6 + hp % 2][:], ACT.Copy).then_inc(attn_hi, 1)
                for lq in range(2):
                    for j in range(SLOTS):
                        residual_tile(Q_EOUT + lq, j, 2, 4 * lq + j)
                        split_hi(Q_EOUT + lq + 1, j, 8)

            def odd_mixer():
                def silu_conv(c):
                    act.wait_ge(conv_step, 3 * c + 3)
                    act.activation(XC[:, c, :], XC[:, c, :], ACT.Silu).then_inc(xc_ready, 1)

                for lq in range(8):
                    for j in range(SLOTS):
                        c = 4 * lq + j
                        act.wait_ge(bank_free, 4 * (Q_OIN + lq) + j + 5)
                        if c < CT:
                            if c == 13:
                                act.wait_ge(prep_ready, 2)
                            act.activation(XC[:, c, :], XM[:, c, :], ACT.Identity, scale=par(C_CONV + 3 * CT + c),
                                           bias=par(C_CONVB + c)).then_inc(tap0, 1)
                        else:
                            act.activation(SZ[:, c - CT, :], GT[:, c % 2, :], ACT.Silu).then_inc(sz_ready, 1)
                        split_hi(Q_OIN + lq + 1, j, 8)
                        if 1 <= c <= CT:
                            silu_conv(c - 1)

                def read(h, name, c, out, **kw):
                    r = ITEM[(h, name, c)]
                    act.wait_ge(item_done, r + 1)
                    ins = act.activation(out, PS[5 + r % 3][:], ACT.Copy, **kw)
                    ins.then_inc(item_read[r % 3], 1)
                    return r

                def gates():
                    act.wait_ge(gate_sum, 1)
                    act.wait_ge(bank_free, 4 * Q_OOUT + 4)
                    act.activation(TMP[0:8, 0, :], AUX[0:8, :], ACT.Identity,
                                   bias=PAR[0:8, C_BG:C_BG + 1]).then_inc(gate_rows, 1)

                def log_sigmoid():
                    act.wait_ge(fg_rows, 1)
                    act.activation(TMP[0:HC, 1, :], PS[0][0:HC, :], ACT.Abs).then_inc(fg_abs, 1)
                    act.wait_ge(fg_abs, 1)
                    link(act.activation(TMP[0:HC, 2, :], TMP[0:HC, 1, :], ACT.Exp, scale=-1.0))
                    act.activation(TMP[0:HC, 3, :], TMP[0:HC, 2, :], ACT.Ln, bias=ones[0:HC, 0:1]).then_inc(log_rows, 1)

                def finish_y(h):
                    for c in range(HT_):
                        act.wait_ge(y_ready, HT_ * h + c + 1)
                        act.activation(YH[:, HT_ * h + c, :], TMP[:, 2 + c, :], ACT.Copy).then_inc(yh_ready, 1)

                def root(h):
                    read_out(act, (h, "ms", 0))
                    act.activation(RSTD[:], RSTD[:], ACT.Sqrt).then_inc(tstd_ready, 1)

                gates()
                for h in range(HC):
                    for c in range(HT_):
                        read(h, "q", c, Q[:, c, :])
                    for c in range(HT_):
                        read(h, "k", c, K[:, c, :], scale=EC ** -0.5)
                    if h == 0:
                        log_sigmoid()
                        act.wait_ge(m_rows, 1)
                        act.activation(EMROW[:], TMP[0:HC, 7, :], ACT.Exp, scale=-1.0).then_inc(em_rows, 1)
                        act.wait_ge(acol_ready, 1)
                        act.wait_ge(em_rows, 1)
                    else:
                        root(h - 1)
                    read(h, "M", 0, TMP[:, 6, :])
                    read_out(act, (h, "M", 0))
                    for j in range(TT):
                        n = TT * h + j
                        if n >= 2:
                            read_out(act, ((n - 2) // TT, "s", (n - 2) % TT))
                        act.activation(TMP[:, j % 2, 0:T - P * j], TMP[:, 6, j * P:], ACT.Exp, scale=-1.0,
                                       bias=ACOL[:, j, h:h + 1]).then_inc(wt_exp, 1)
                    if h:
                        finish_y(h - 1)
                    act.wait_ge(num_done, h + 1)
                    act.activation(RSTD[:], PS[4][:], ACT.Abs).then_inc(den_abs, 1)
                    for c in range(HT_):
                        if c == 3:
                            act.wait_ge(ssq_step, 3 * h + 1)
                        act.activation((SQ[:], SQX[:], TMP[:, 6, :], SQX[:])[c], PS[c][:],
                                       ACT.Square).then_inc(num_sq, 1)
                root(HC - 1)
                finish_y(HC - 1)
                for lq in range(4):
                    for j in range(SLOTS):
                        residual_tile(Q_OOUT + lq, j, 5 if lq >= 2 else None, 4 * (lq % 2) + j)
                        split_hi(Q_OOUT + lq + 1, j, 8)

            act.wait_ge(par_in, 32)
            for h in range(HA):
                act.wait_ge(bias_sum, 2 * h + 1)
                act.activation(STG[:, h, 0:T], PS[6][:], ACT.Copy).then_inc(bias_staged, 1)
                act.wait_ge(bias_sum, 2 * h + 2)
                act.activation(STG[:, h, T:BW], PS[7][:, 0:P], ACT.Copy).then_inc(bias_staged, 1)
            act.wait_ge(x_in, 16)
            for m in range(KX):
                new_x_tile(0, m)
                if m % 2:
                    split_hi(0, m // 2, 8)
            act.wait_ge(small_ready, 1)
            norm(0)
            ffn(0, Q_FFN[0], 1, True)
            norm(1)
            even_mixer()
            norm(2)
            ffn(1, Q_FFN[1], 3, True)
            norm(3)
            ffn(2, Q_FFN[2], 4, True)
            norm(4)
            odd_mixer()
            norm(5)
            ffn(3, Q_FFN[3], None, False)

        @block.vector
        def _(dve):
            steps = [0]

            def link(ins):
                steps[0] += 1
                ins.then_inc(vector_step, 1)
                dve.wait_ge(vector_step, steps[0])

            def split_lo(q, j, kt):
                dve.wait_ge(hi_ready, 4 * q + j + 1)
                dve.tensor_tensor(LO[j][:, 0:kt * P], RAW[j][:, 0:kt * P], HI[j][:, 0:kt * P].bitcast(F32),
                                  ALU.subtract).then_inc(lo_ready, 1)

            def new_x_tile(r, m):
                dve.wait_ge(xh_ready, 8 * r + m + 1)
                dve.scalar_tensor_tensor(XL[:, m, :], X[:, m, :], par(C_NORM + 8 * r + m), XH[:, m, :].bitcast(F32),
                                         ALU.mult, ALU.subtract).then_inc(xl_ready, 1)

            def norm(r):
                dve.wait_ge(std_ready, r + 1)
                dve.reciprocal(RSTD[:], RSTD[:]).then_inc(rstd_ready, 1)
                dve.wait_ge(rstd_ready, r + 1)

            def scaled(q, j, out):
                dve.wait_ge(unit_done, 4 * q + j + 1)
                dve.tensor_tensor(out, PS[j][:], RSTD[:], ALU.mult).then_inc(bank_free, 1)

            def residual_tile(q, j, r, m, factor):
                dve.wait_ge(unit_done, 4 * q + j + 1)
                dve.scalar_tensor_tensor(X[:, m, :], PS[j][:], factor, X[:, m, :], ALU.mult,
                                         ALU.add).then_inc(bank_free, 1)
                if r is not None:
                    new_x_tile(r, m)

            def ffn(f, q0, r, after):
                def step(third, lq, last):
                    q = q0 + 6 * third + lq
                    for j in range(SLOTS):
                        if is_gate_up(lq, last):
                            m = 2 * lq + j // 2
                            if j % 2 == 0:
                                scaled(q, j, GT[:, m % 2, :])
                            else:
                                dve.wait_ge(sr_ready, 22 * f + 8 * third + (m + 1))
                                dve.wait_ge(unit_done, 4 * q + j + 1)
                                dve.tensor_tensor(HT[:, m % 2, :], PS[j][:], SR[:, m % 2, :],
                                                  ALU.mult).then_inc(bank_free, 1)
                        else:
                            residual_tile(q, j, r if last else None, 4 * (lq - (3 if last else 4)) + j, 0.5)
                        if last and lq >= 2:
                            if lq < 4:
                                split_lo(q + 1, j, 6)
                            elif after:
                                split_lo(q + 1, j, 8)
                        else:
                            split_lo(q + 1, j, 8)
                walk_ffn(dve, step)

            def even_mixer():
                for lq in range(4):
                    for j in range(SLOTS):
                        u = 4 * lq + j
                        scaled(Q_EIN + lq, j, QK[:, u, :] if u < 8 else TMP[:, u - 8, :] if u < 12
                               else U[:, u - 12, PAD:])
                        split_lo(Q_EIN + lq + 1, j, 8)
                dve.wait_ge(row_std, 1)
                dve.reciprocal(RSTD[0:16, :], RSTD[0:16, :]).then_inc(row_rstd, 1)
                for n, m in enumerate((0, 4, 1, 5, 2, 6, 3, 7)):
                    dve.wait_ge(qk_bcast, n + 1)
                    dve.scalar_tensor_tensor(QK[:, m, :], QK[:, m, :], QG[:] if m < 4 else par(C_KG),
                                             PS[4 + n % 2][:], ALU.mult, ALU.mult).then_inc(qk_normed, 1)

                def shifted(a):
                    hp, i, half = ROWS[a]
                    n = (i + 1) * P
                    dve.wait_ge(s_done, a + 1)
                    if a >= 2:
                        dve.wait_ge(p_exp, a - 1)
                    else:
                        dve.wait_ge(v_turned, 4)
                    dve.tensor_tensor_reduce(TMP[:, a % 2, 0:n], PS[a % 2][:, 0:n],
                                             G[:, 2 * hp + half, T - n:T], -1.0, 3.0e38, ALU.add, ALU.min,
                                             ATT[:, 0, a:a + 1]).then_inc(s_shift, 1)

                def normed(a):
                    _, i, _ = ROWS[a]
                    n = (i + 1) * P
                    dve.wait_ge(p_exp, a + 1)
                    dve.reciprocal(ATT[:, 2, a:a + 1], ATT[:, 1, a:a + 1]).then_inc(p_inv, 1)
                    dve.wait_ge(p_inv, a + 1)
                    dve.tensor_scalar(TMP[:, 2 + a % 3, 0:n], TMP[:, 2 + a % 3, 0:n], ATT[:, 2, a:a + 1], None,
                                      ALU.mult).then_inc(p_ready, 1)

                dve.wait_ge(skew_in, 16 * HA)
                for a in range(len(ROWS) + 6):
                    if a < len(ROWS):
                        shifted(a)
                    if 1 <= a <= len(ROWS):
                        normed(a - 1)
                    if a - 3 in POOL_AT:
                        g = POOL_AT[a - 3]
                        dve.wait_ge(pool_hi, g + 1)
                        dve.scalar_tensor_tensor(HL[:, 4 + g, :], PS[4 + g % 2][:], par(C_PSC + g),
                                                 HH[:, 4 + g, :].bitcast(F32), ALU.mult,
                                                 ALU.subtract).then_inc(pool_lo, 1)
                    if a >= 13 and (a - 13) % 8 == 0:
                        hp = (a - 13) // 8
                        dve.wait_ge(attn_hi, hp + 1)
                        dve.tensor_tensor(HL[:, hp, :], PS[6 + hp % 2][:], HH[:, hp, :].bitcast(F32),
                                          ALU.subtract).then_inc(attn_lo, 1)
                for lq in range(2):
                    for j in range(SLOTS):
                        residual_tile(Q_EOUT + lq, j, 2, 4 * lq + j, 1.0)
                        split_lo(Q_EOUT + lq + 1, j, 8)

            def odd_mixer():
                def conv(c):
                    dve.wait_ge(tap0, c + 1)
                    for n, back in enumerate((1, 2, 3)):
                        if n:
                            dve.wait_ge(conv_step, 3 * c + n)
                        dve.scalar_tensor_tensor(XC[:, c, back:], XM[:, c, 0:T - back],
                                                 par(C_CONV + (TAPS - 1 - back) * CT + c), XC[:, c, back:],
                                                 ALU.mult, ALU.add).then_inc(conv_step, 1)

                for lq in range(8):
                    for j in range(SLOTS):
                        c = 4 * lq + j
                        if c >= CT + 2:
                            dve.wait_ge(sz_ready, c - CT - 1)
                        scaled(Q_OIN + lq, j, XM[:, c, :] if c < CT else GT[:, c % 2, :])
                        if 1 <= c <= CT:
                            conv(c - 1)
                        split_lo(Q_OIN + lq + 1, j, 8)

                def gate_rows():
                    dve.wait_ge(fg_abs, 1)
                    link(dve.tensor_scalar(TMP[0:HC, 4, :], PS[0][0:HC, :], 0.0, None, ALU.min))
                    dve.wait_ge(log_rows, 1)
                    link(dve.tensor_tensor(TMP[0:HC, 4, :], TMP[0:HC, 4, :], TMP[0:HC, 3, :], ALU.subtract))
                    link(dve.tensor_tensor_scan(TMP[0:HC, 5, :], ones[0:HC, 0:1].to_broadcast([HC, T]), TMP[0:HC, 4, :], 0.0, ALU.mult, ALU.add))
                    dve.tensor_tensor(TMP[0:HC, 6, :], TMP[0:HC, 0, :], TMP[0:HC, 5, :],
                                      ALU.subtract).then_inc(a_rows, 1)
                    dve.wait_ge(a_rows, 1)
                    link(dve.tensor_tensor_scan(MROW[:], TMP[0:HC, 6, :], TMP[0:HC, 6, :], 0.0, ALU.max, ALU.max))
                    dve.tensor_tensor(TMP[0:HC, 7, :], TMP[0:HC, 5, :], MROW[:], ALU.add).then_inc(m_rows, 1)

                def item(h, name, c):
                    r = ITEM[(h, name, c)]
                    dve.wait_ge(item_done, r + 1)
                    return PS[5 + r % 3], item_read[r % 3]

                def squares(h):
                    for n, other in enumerate((SQX[:], TMP[:, 6, :], SQX[:])):
                        dve.wait_ge(num_sq, 4 * h + n + 2)
                        if n:
                            dve.wait_ge(ssq_step, 3 * h + n)
                        dve.tensor_tensor(SQ[:], SQ[:], other, ALU.add).then_inc(ssq_step, 1)
                    dve.wait_ge(den_abs, h + 1)
                    link(dve.tensor_tensor(RSTD[:], RSTD[:], TMP[:, 7, :], ALU.max))
                    link(dve.scalar_tensor_tensor(RSTD[:], RSTD[:], EPS, RSTD[:], ALU.mult, ALU.mult))

                def head_factor(h):
                    ps, read = item(h, "ms", 0)
                    dve.scalar_tensor_tensor(RSTD[:], ps[:], 1.0 / EC, RSTD[:], ALU.mult, ALU.add).then_inc(read, 1)

                def scale_numerator(h):
                    dve.wait_ge(tstd_ready, h + 1)
                    link(dve.reciprocal(RSTD[:], RSTD[:]))
                    for c in range(HT_):
                        if h:
                            dve.wait_ge(yl_ready, HT_ * (h - 1) + c + 1)
                        dve.scalar_tensor_tensor(TMP[:, 2 + c, :], PS[c][:], par(C_GAIN + HT_ * h + c), RSTD[:],
                                                 ALU.mult, ALU.mult).then_inc(num_read, 1)

                def add_skip(h):
                    for c in range(HT_):
                        ch = HT_ * h + c
                        dve.wait_ge(num_read, ch + 1)
                        dve.scalar_tensor_tensor(TMP[:, 2 + c, :], XC[:, ch, :], par(C_SKIP + ch), TMP[:, 2 + c, :],
                                                 ALU.mult, ALU.add).then_inc(y_pre, 1)

                for h in range(HC):
                    if h == 0:
                        gate_rows()
                    else:
                        squares(h - 1)
                        head_factor(h - 1)
                    for c in range(HT_):
                        ps, read = item(h, "v", c)
                        dve.tensor_copy(XM[:, HT_ * h + c, :], ps[:]).then_inc(read, 1)
                    if h == 0:
                        dve.wait_ge(a_turned, 1)
                        dve.tensor_copy(ACOL[:].rearrange("p j h -> p (j h)"),
                                        PS[1][:, 0:TT * HC]).then_inc(acol_ready, 1)
                    ps, read = item(h, "EM", 0)
                    dve.tensor_copy(TMP[:, 7, :], ps[:]).then_inc(read, 1)
                    if h:
                        scale_numerator(h - 1)
                    for j in range(TT):
                        dve.wait_ge(wt_ready, TT * h + j + 1)
                        ps, read = item(h, "s", j)
                        n = T - P * j
                        dve.tensor_tensor(PT[:, j, 0:n], ps[:, 0:n], TMP[:, j % 2, 0:n], ALU.mult).then_inc(read, 1)
                    if h:
                        add_skip(h - 1)
                squares(HC - 1)
                head_factor(HC - 1)
                scale_numerator(HC - 1)
                add_skip(HC - 1)
                for lq in range(4):
                    for j in range(SLOTS):
                        residual_tile(Q_OOUT + lq, j, 5 if lq >= 2 else None, 4 * (lq % 2) + j, 1.0)
                        split_lo(Q_OOUT + lq + 1, j, 8)

            dve.memset(EPST[:], EPS).then_inc(small_ready, 1)
            dve.wait_ge(par_in, 32)
            dve.tensor_scalar(QG[:], par(C_QG), EA ** -0.5, None, ALU.mult).then_inc(bank_free, SLOTS)
            dve.wait_ge(x_in, 16)
            for m in range(KX):
                new_x_tile(0, m)
                if m % 2:
                    split_lo(0, m // 2, 8)
            norm(0)
            ffn(0, Q_FFN[0], 1, True)
            norm(1)
            even_mixer()
            norm(2)
            ffn(1, Q_FFN[1], 3, True)
            norm(3)
            ffn(2, Q_FFN[2], 4, True)
            norm(4)
            odd_mixer()
            norm(5)
            ffn(3, Q_FFN[3], None, False)

        @block.gpsimd
        def _(pool):
            steps = [0]

            def link(ins):
                steps[0] += 1
                ins.then_inc(pool_step, 1)
                pool.wait_ge(pool_step, steps[0])

            def square_tile(r, m):
                pool.wait_ge(sqt_ready, 8 * r + m + 1)
                if m:
                    pool.wait_ge(sq_ready, 8 * r + m)
                    pool.tensor_tensor(SQ[:], SQ[:], GT[:, m % 2, :], ALU.add).then_inc(sq_ready, 1)
                else:
                    pool.tensor_copy(SQ[:], GT[:, 0, :]).then_inc(sq_ready, 1)

            def ffn(f, q0, r):
                def step(third, lq, last):
                    if is_gate_up(lq, last):
                        for m in (2 * lq, 2 * lq + 1):
                            pair = 22 * f + 8 * third + (m + 1)
                            pool.wait_ge(silu_ready, pair)
                            pool.tensor_tensor(SR[:, m % 2, :], SG[:, m % 2, :], RSTD[:], ALU.mult).then_inc(sr_ready, 1)
                            pool.wait_ge(hh_ready, pair)
                            pool.tensor_tensor(HL[:, m, :], HT[:, m % 2, :], HH[:, m, :].bitcast(F32),
                                               ALU.subtract).then_inc(hl_ready, 1)
                    elif last and r is not None:
                        for j in range(SLOTS):
                            square_tile(r, 4 * (lq - 3) + j)
                walk_ffn(pool, step)

            def pool_group(g):
                pool.wait_ge(bank_free, 4 * (Q_EIN + 3) + g + 5)
                x = U[:, g, :]
                width, src = 1, x
                for n in range(g + 1):
                    dst = WSUM[:, n % 2, :]
                    link(pool.tensor_tensor(dst[:, PAD:], src[:, PAD:], src[:, PAD - width:PAD + T - width], ALU.add))
                    width, src = 2 * width, dst
                mean = src[:, PAD:]
                link(pool.tensor_scalar(mean, mean, 1.0 / WINDOWS[g], None, ALU.mult))
                link(pool.tensor_tensor(mean[:, 0:16], mean[:, 0:16], CST[:, K_FIX + 16 * g:K_FIX + 16 * g + 16],
                                        ALU.mult))
                pool.tensor_tensor(x[:, PAD:], mean, x[:, PAD:], ALU.subtract).then_inc(diff_ready, 1)
                pool.wait_ge(diff_ready, g + 1)

            def gate_weights():
                pool.wait_ge(prep_in, 64)
                flat = [CT, 4, 2 * HC]
                for t in range(3):
                    last = pool.tensor_tensor(WGR[:, t], WGR[:, t], W3[:, t].unsqueeze(3).to_broadcast([P] + flat),
                                              ALU.mult)
                link(last)
                link(pool.tensor_tensor(WGR[:, 0], WGR[:, 0], WGR[:, 1], ALU.add))
                for n, t in enumerate((0, 2)):
                    out = WP[:, n * CT:(n + 1) * CT, :]
                    link(pool.tensor_tensor(out, WGR[:, t, :, 0, :], WGR[:, t, :, 1, :], ALU.add))
                    link(pool.tensor_tensor(out, out, WGR[:, t, :, 2, :], ALU.add))
                    pool.tensor_tensor(out, out, WGR[:, t, :, 3, :], ALU.add).then_inc(prep_ready, 1)

            def block_diagonals(h):
                if h:
                    pool.wait_ge(item_done, ITEM[(h - 1, "v", HT_ - 1)] + 1)
                else:
                    pool.wait_ge(bank_free, 4 * Q_OOUT + 4)
                mask = CST[:, K_MASK:K_MASK + 32].unsqueeze(1).unsqueeze(3).to_broadcast([P, HT_, 32, 4])
                for t in range(3):
                    w = W3[:, t, HT_ * h:HT_ * h + HT_, :].unsqueeze(2).to_broadcast([P, HT_, 32, 4])
                    last = pool.tensor_tensor(BD[:, t].rearrange("p c (g o) -> p c g o", g=32), w, mask, ALU.mult)
                last.then_inc(bd_ready, 1)

            def outputs(h):
                for c in range(HT_):
                    n = HT_ * h + c
                    pool.wait_ge(y_pre, n + 1)
                    pool.wait_ge(sz_ready, n + 1)
                    pool.tensor_tensor(TMP[:, 2 + c, :], TMP[:, 2 + c, :], SZ[:, n, :], ALU.mult).then_inc(y_ready, 1)
                for c in range(HT_):
                    n = HT_ * h + c
                    pool.wait_ge(yh_ready, n + 1)
                    pool.tensor_tensor(YL[:, n, :], TMP[:, 2 + c, :], YH[:, n, :].bitcast(F32),
                                       ALU.subtract).then_inc(yl_ready, 1)

            pool.memset(U[:, :, 0:PAD], 0.0)
            link(pool.memset(WSUM[:, :, 0:PAD], 0.0))
            for m in range(KX):
                square_tile(0, m)
            ffn(0, Q_FFN[0], 1)
            for g in range(NG):
                pool_group(g)
            for m in range(KX):
                square_tile(2, m)
            ffn(1, Q_FFN[1], 3)
            ffn(2, Q_FFN[2], 4)
            gate_weights()
            block_diagonals(0)
            for h in range(HC):
                for j in range(TT):
                    n = TT * h + j
                    pool.wait_ge(wt_exp, n + 1)
                    pool.affine_select(TMP[:, j % 2, 0:P], TMP[:, j % 2, 0:P], pattern=[[1, P]],
                                       compare_op=ALU.is_ge, fill=0.0, base=0,
                                       channel_multiplier=-1).then_inc(wt_ready, 1)
                if h + 1 < HC:
                    block_diagonals(h + 1)
                if h:
                    outputs(h - 1)
            outputs(HC - 1)
            for m in range(KX):
                square_tile(5, m)
            ffn(3, Q_FFN[3], None)



def tiles(w):
    i, o = w.shape
    return w.reshape(i // P, P, o // P, P).transpose(2, 1, 0, 3).reshape(o // P, P, (i // P) * P)


def lay_out(a):
    w = {}
    w["xT"] = a["x"][0].T.reshape(KX, P, T).transpose(1, 0, 2)
    gate, up, down = (a[n].reshape((NFFN,) + a[n].shape[2:]) for n in ("ffn_w_gate", "ffn_w_up", "ffn_w_down"))
    w["gu"] = np.stack([np.stack([tiles(gate[f]), tiles(up[f])], 1).reshape(2 * FT, P, KMAX * P) for f in range(NFFN)])
    w["down"] = np.stack([np.concatenate([tiles(down[f][t * 1024:t * 1024 + 1024]) for t in range(2)])
                          for f in range(NFFN)])
    w["down2"] = np.stack([tiles(down[f][2048:]) for f in range(NFFN)])
    w["ein"] = tiles(a["ev_w_in"][0])
    w["eout"] = tiles(a["ev_w_out"][0])
    w["oin"] = tiles(a["od_w_in"][0])
    w["oout"] = np.concatenate([tiles(a["od_w_out"][0][t * 1024:t * 1024 + 1024]) for t in range(2)])
    column = lambda v: v.reshape(-1, P).T
    bias = np.zeros((P, 1), np.float32)
    bias[0:2 * HC, 0] = a["od_b_gates"][0]
    w["par"] = np.concatenate([
        a["norm_gains"].reshape(6, KX, P).transpose(2, 0, 1).reshape(P, 48),
        a["od_conv_w"][0].reshape(TAPS, CT, P).transpose(2, 0, 1).reshape(P, TAPS * CT),
        column(a["od_conv_b"][0]), column(a["od_skip"][0]), column(a["od_out_gain"][0]), column(a["ev_pool_scale"][0]),
        np.tile(a["ev_q_gain"][0], 2)[:, None], np.tile(a["ev_k_gain"][0], 2)[:, None], bias], 1)
    w["cst"], w["hot"], w["pick"] = shape_constants()
    w["relb"] = np.concatenate([a["rel_bias"], np.ones((1, HA), np.float32)])
    w["w3"] = np.stack([a[n][0].reshape(CT, P, 4).transpose(1, 0, 2) for n in ("od_wq", "od_wk", "od_wv")], 1)
    gates = a["od_w_gates"][0].reshape(3, CT, P // 4, 1, 4, 2 * HC)
    w["wgr"] = np.broadcast_to(gates, (3, CT, P // 4, 4, 4, 2 * HC)).transpose(2, 3, 0, 1, 4, 5).reshape(P, -1)
    w["poolw"] = a["ev_pool_w"][0].transpose(1, 0, 2)
    return {n: np.ascontiguousarray(v) for n, v in w.items()}


def kernel(**inputs):
    import concourse.bacc as bacc
    from concourse.bass_utils import run_bass_kernel_spmd

    w = lay_out({n: np.asarray(v) for n, v in inputs.items()})
    nc = bacc.Bacc("TRN2", target_bir_lowering=False, num_devices=1)
    names = ["xT", "par", "cst", "hot", "relb", "w3", "wgr", "poolw", "pick", "gu", "down", "down2", "ein", "eout", "oin", "oout"]
    arrays = {n + "_dram": w[n] for n in names}
    args = [nc.dram_tensor(n + "_dram", w[n].shape, F32, kind="ExternalInput").ap() for n in names]
    args.append(nc.dram_tensor("skew_dram", (HA, P, BW), F32, kind="Internal").ap())
    args.append(nc.dram_tensor("out_dram", (P, KX, T), F32, kind="ExternalOutput").ap())
    trunk(nc, *args)
    r = run_bass_kernel_spmd(nc, [arrays], core_ids=[0])
    out = r.results[0]["out_dram"]
    return out.transpose(1, 0, 2).reshape(DM, T).T.reshape(1, T, DM)
```

```python
import math
from contextlib import ExitStack

import numpy as np

import concourse.bass as bass
from concourse import mybir

F32 = mybir.dt.float32
F32R = mybir.dt.float32r
ACT = mybir.ActivationFunctionType
ALU = mybir.AluOpType

P = 128
T = 512
DM = 1024
KX = DM // P
NFFN = 4
FF = 2816
FT = FF // P
SLOTS = 4
KMAX = 8
EPS = 1e-6

HA, EA = 8, 64
NG = 4
WINDOWS = (2, 4, 8, 16)
PAD = 16
PATTERNS = ((128, 1), (512, 4), (2048, 16))
BUCKETS, MAX_DISTANCE = 32, 2048
BW = T + P
NEG = -2.0 ** 100

HC = 4
INNER = 2 * DM
CT = INNER // P
HT_ = CT // HC
EC = INNER // HC
TAPS = 4
TT = T // P

FFN_QUADS = 17
Q_FFN = (0, 23, 40, 69)
Q_EIN, Q_EOUT = 17, 21
Q_OIN, Q_OOUT = 57, 65
Q_END = 86
GATE_UNIT = 8

C_NORM, C_CONV, C_CONVB, C_SKIP, C_GAIN, C_PSC, C_QG, C_KG, C_BG = 0, 48, 112, 128, 144, 160, 164, 165, 166
NPAR = 167
K_ID, K_ONE, K_HS, K_MASK, K_FIX, K_SEL, K_ROW = 0, 128, 256, 384, 416, 480, 516
NCST = 521


def t5_bucket(d):
    exact = BUCKETS // 2
    f = np.maximum(d.astype(np.float32), np.float32(1))
    large = exact + (np.log(f / exact) / np.float32(math.log(MAX_DISTANCE / exact)) * (BUCKETS - exact)).astype(np.int32)
    return np.where(d < exact, d, np.minimum(large, BUCKETS - 1))


def shape_constants():
    c = np.zeros((P, NCST), np.float32)
    c[:, K_ID:K_ID + P] = np.eye(P)
    c[:, K_ONE:K_ONE + P] = 1
    for m in range(8):
        for half in range(2):
            c[64 * half:64 * half + 64, K_HS + 16 * m + 2 * m + half] = 1
    for g in range(32):
        c[4 * g:4 * g + 4, K_MASK + g] = 1
    for g, w in enumerate(WINDOWS):
        c[:, K_FIX + 16 * g:K_FIX + 16 * g + 16] = w / np.minimum(np.arange(1, 17), w)
    for i in range(HC):
        c[[i, 2 * HC + i], K_SEL + i] = 1
        c[[HC + i, 3 * HC + i], K_SEL + 32 + i] = 1
        c[[i, 32 + i], K_ROW + i] = 1
    c[:, K_ROW + HC] = 1
    d = T - 1 - np.arange(BW)
    hot = np.zeros((P, BW), np.float32)
    log_count = np.full(BW, NEG, np.float32)
    count = np.zeros(BW)
    for window, dilation in PATTERNS:
        count += (d >= 0) & (d <= window) & (d % dilation == 0)
    b = t5_bucket(np.maximum(d, 0))
    for z in range(BW):
        if count[z]:
            hot[b[z], z] = 1
            log_count[z] = math.log(count[z])
    hot[BUCKETS] = (log_count.view(np.uint32) & np.uint32(0xFFFFF000)).view(np.float32)
    hot[BUCKETS + 1] = log_count - hot[BUCKETS]
    pick = np.zeros((P, 8 * P), np.float32)
    pick[0:16] = np.concatenate([c[:, K_HS + 16 * m:K_HS + 16 * m + 16].T for m in range(8)], 1)
    return c, hot, pick


def core_items():
    items = []
    for h in range(HC):
        if h == 0:
            items.append((0, "A", 0))
        items += [(h, "q", c) for c in range(HT_)]
        items += [(h, "v", 0), (h, "v", 1)]
        if h:
            items.append((h - 1, "ms", 0))
        items += [(h, "v", 2), (h, "M", 0), (h, "EM", 0), (h, "v", 3)]
        items += [(h, "s", j) for j in range(TT)]
        if h + 1 < HC:
            items.append((h + 1, "A", 0))
    items.append((HC - 1, "ms", 0))
    return {item: r for r, item in enumerate(items)}


def trunk(nc, xT, par_d, cst_d, hot_d, relb_d, w3_d, wgr_d, poolw_d, pick_d, gu_d, down_d, down2_d, ein_d, eout_d,
          oin_d, oout_d, skew_d, out_d):
    ctx = ExitStack()
    with ctx:
        def sb(name, shape, dt=F32):
            return ctx.enter_context(nc.sbuf_tensor(name, shape, dt))

        def sem(name):
            return ctx.enter_context(nc.semaphore(name))

        X = sb("X", [P, KX, T])
        RSTD = sb("RSTD", [P, T])
        SQ = sb("SQ", [P, T])
        PAR = sb("PAR", [P, NPAR])
        CST = sb("CST", [P, NCST])
        W3 = sb("W3", [P, 5, CT, 4])
        WP = sb("WP", [P, 2 * CT, 2 * HC])
        EPST = sb("EPST", [P, 1])
        QG = sb("QG", [P, 1])
        ATT = sb("ATT", [P, 3, 4 * HA])
        ACOL = sb("ACOL", [P, TT, HC])
        WPS = sb("WPS", [P, 2 * CT, 4 * HC], F32R)
        SELR = sb("SELR", [P, HC + 1], F32R)
        RBH = sb("RBH", [P, HA], F32R)
        RBL = sb("RBL", [P, HA], F32R)

        def region(name, nbytes):
            base = nc.sbuf_base
            sb(name, [P, nbytes // 4])
            return base

        TB = T * 4
        ring0 = region("ring", 2 * SLOTS * KMAX * P * 4)
        xr0 = region("x_region", 16 * TB)
        hr0 = region("h_region", 16 * TB)
        e0 = region("mixer_region", 34 * TB)
        tmp0 = region("tmp_region", 8 * TB)

        def at(name, shape, base, offset, dt=F32):
            return nc.alloc_sbuf_tensor_at(name, shape, dt, offset=base + offset)

        SB = KMAX * P * 4
        RAW = [at(f"RAW{s}", [P, KMAX * P], ring0, 2 * s * SB) for s in range(SLOTS)]
        LO = [at(f"LO{s}", [P, KMAX * P], ring0, 2 * s * SB, F32R) for s in range(SLOTS)]
        HI = [at(f"HI{s}", [P, KMAX * P], ring0, (2 * s + 1) * SB, F32R) for s in range(SLOTS)]
        TMP = at("TMP", [P, 8, T], tmp0, 0)
        XH = at("XH", [P, KX, T], xr0, 0, F32R)
        XL = at("XL", [P, KX, T], xr0, 8 * TB, F32R)
        HH = at("HH", [P, 8, T], hr0, 0, F32R)
        HL = at("HL", [P, 8, T], hr0, 8 * TB, F32R)
        STG = at("STG", [P, HA, BW], e0, 0)
        RELB = at("RELB", [P, HA], e0, 20480)
        HOT = at("HOT", [P, BW], e0, 20544)
        HOTR = at("HOTR", [P, BW], e0, 20544, F32R)
        QK = at("QK", [P, 8, T], e0, 0)
        SQB = at("SQB", [P, 8, T], e0, 8 * TB)
        V = SQB
        G = at("G", [P, HA, T], e0, 16 * TB)
        U = at("U", [P, NG, PAD + T], e0, 24 * TB)
        WSUM = at("WSUM", [P, 2, PAD + T], e0, 24 * TB + NG * (PAD + T) * 4)
        POOLW = at("POOLW", [P, NG, P], e0, 31 * TB)
        QZ = [at(f"QZ{half}", [P, 4, T], hr0, 8 * TB * half) for half in range(2)]
        ROWH = at("ROWH", [P, T], tmp0, 5 * TB, F32R)
        ROWL = at("ROWL", [P, T], tmp0, 6 * TB, F32R)
        PICK = at("PICK", [P, 8 * P], e0, 32 * TB)
        PICKR = at("PICKR", [P, 8 * P], e0, 32 * TB, F32R)
        WGR = at("WGR", [P, 3, CT, 4, 2 * HC], e0, 29 * TB)
        XM = at("XM", [P, CT, T], e0, 0)
        XC = at("XC", [P, CT, T], e0, CT * TB)
        MEM = at("MEM", [P, 2, T], e0, 2 * CT * TB, F32R)
        GXH = at("GXH", [P, 2, T], tmp0, 2 * TB, F32R)
        GXL = at("GXL", [P, 2, T], tmp0, 4 * TB, F32R)
        BD0 = at("BD0", [P, 3, HT_, P], tmp0, 5 * TB)
        YH = at("YH", [P, CT, T], e0, 0, F32R)
        YL = at("YL", [P, CT, T], e0, CT * TB, F32R)
        SZ = at("SZ", [P, CT, T], hr0, 0)
        Q = at("Q", [P, HT_, T], xr0, 0)
        AM = at("AM", [P, HT_, P], xr0, 4 * TB)
        AM0 = at("AM0", [P, HT_, P], tmp0, 2 * TB)
        PO = [0] + [sum(T - P * i for i in range(j)) for j in range(1, TT + 1)]
        PTL = at("PTL", [P, PO[TT]], xr0, 5 * TB, F32R)
        PTH = at("PTH", [P, PO[TT]], xr0, 8 * TB, F32R)
        VH = at("VH", [P, CT, T], e0, 0, F32R)
        VL = at("VL", [P, HT_, T], ring0, 6 * SB, F32R)
        BD = at("BD", [P, 3, HT_, P], xr0, 12 * TB)
        SQX = at("SQX", [P, T], xr0, 15 * TB)

        GT, SG, SR, HT = (TMP[:, 2 * i:2 * i + 2, :] for i in range(4))

        ident = CST[:, K_ID:K_ID + P]
        ones = CST[:, K_ONE:K_ONE + P]

        def par(col):
            return PAR[:, col:col + 1]

        PS = [ctx.enter_context(nc.psum_tensor(f"PS{b}", [P, T], F32)) for b in range(8)]
        AUX = PS[4]

        x_in = [sem(f"x_in{c}") for c in range(4)]
        par_in, cst_in, hot_in, skew_out, skew_in, prep_in, out_done = (
            sem(n) for n in ("par_in", "cst_in", "hot_in", "skew_out", "skew_in", "prep_in", "out_done"))
        weights_in = [sem(f"weights_in{s}") for s in range(SLOTS)]
        hi_ready, lo_ready, unit_done = sem("hi_ready"), sem("lo_ready"), sem("unit_done")
        bank_free = sem("bank_free")
        silu_ready, sr_ready, hh_ready, hl_ready = (sem(n) for n in ("silu_ready", "sr_ready", "hh_ready", "hl_ready"))
        xh_ready, xl_ready, sqt_ready, sq_ready = (sem(n) for n in ("xh_ready", "xl_ready", "sqt_ready", "sq_ready"))
        norm_sum, std_ready, rstd_ready = sem("norm_sum"), sem("std_ready"), sem("rstd_ready")
        small_ready = sem("small_ready")
        bias_ready, bias_sum, bias_staged = sem("bias_ready"), sem("bias_sum"), sem("bias_staged")
        rows_clear, row_hi, row_lo, pick_ready, qz_clear = (
            sem(n) for n in ("rows_clear", "row_hi", "row_lo", "pick_ready", "qz_clear"))
        gate_hi, gate_lo, wps_hi, wps_lo, mem_clear = (
            sem(n) for n in ("gate_hi", "gate_lo", "wps_hi", "wps_lo", "mem_clear"))
        qk_sq, qk_rows, row_std, row_rstd, qk_bcast, qk_normed = (
            sem(n) for n in ("qk_sq", "qk_rows", "row_std", "row_rstd", "qk_bcast", "qk_normed"))
        v_turned, v_ready = sem("v_turned"), sem("v_ready")
        s_done, s_shift, p_exp, p_inv, p_ready, pt_done, pt_ready, pv_done = (
            sem(n) for n in ("s_done", "s_shift", "p_exp", "p_inv", "p_ready", "pt_done", "pt_ready", "pv_done"))
        attn_hi, attn_lo, diff_ready, pool_mm, pool_hi, pool_lo = (
            sem(n) for n in ("attn_hi", "attn_lo", "diff_ready", "pool_mm", "pool_hi", "pool_lo"))
        tap0, conv_step, xc_ready, sz_ready, prep_ready = (
            sem(n) for n in ("tap0", "conv_step", "xc_ready", "sz_ready", "prep_ready"))
        gate_sum, gate_rows, fg_rows, fg_abs, log_rows = (
            sem(n) for n in ("gate_sum", "gate_rows", "fg_rows", "fg_abs", "log_rows"))
        a_rows, m_rows, mem_hi, mem_lo, sel_ready, a_turned, acol_ready = (
            sem(n) for n in ("a_rows", "m_rows", "mem_hi", "mem_lo", "sel_ready", "a_turned", "acol_ready"))
        bd_ready, item_done = sem("bd_ready"), sem("item_done")
        item_read = [sem(f"item_read{b}") for b in range(3)]
        wt_exp, wt_ready = sem("wt_exp"), sem("wt_ready")
        vh_ready, pth_ready, ptl_ready = sem("vh_ready"), sem("pth_ready"), sem("ptl_ready")
        num_done, den_abs, num_sq, ssq_step, tstd_ready, num_read = (
            sem(n) for n in ("num_done", "den_abs", "num_sq", "ssq_step", "tstd_ready", "num_read"))
        y_pre, y_ready, yh_ready, yl_ready = (sem(n) for n in ("y_pre", "y_ready", "yh_ready", "yl_ready"))
        vector_step, scalar_step, pool_step = sem("vector_step"), sem("scalar_step"), sem("pool_step")

        ITEM = core_items()
        OUT_BANKS = (4, 6, 7, 5)
        ROWS = [(hp, i, half) for hp in range(HA // 2) for i in range(TT) for half in range(2)]
        POOL_AT = {6 + 4 * g: g for g in range(NG)}

        def read_out(eng, item):
            r = ITEM[item]
            eng.wait_ge(item_read[r % 3], r // 3 + 1)

        def read_through(eng, item):
            for r in range(ITEM[item] - 2, ITEM[item] + 1):
                eng.wait_ge(item_read[r % 3], r // 3 + 1)

        def walk_ffn(eng, step):
            with eng.Fori(0, 2) as third:
                for lq in range(6):
                    step(third, lq, False)
            for lq in range(5):
                step(2, lq, True)

        def is_gate_up(lq, last):
            return lq < (3 if last else 4)

        block = ctx.enter_context(nc.Block())

        @block.sync
        def _(sp):
            def load(q, j, src):
                sp.wait_ge(unit_done, 4 * q + j - 3)
                sp.dma_start(RAW[j][:, 0:src.shape[1]], src).then_inc(weights_in[j], 16)

            def ffn(f, q0, after):
                def step(third, lq, last):
                    q = q0 + 6 * third + lq + 1
                    for j in range(SLOTS):
                        if last and lq == 4:
                            if after is not None:
                                load(q, j, after[j])
                        elif last:
                            if f == 0 and lq == 3 and j == 0:
                                sp.wait_ge(bias_staged, 2 * HA)
                                sp.dma_start(skew_d.rearrange("h p z -> p h z"), STG[:]).then_inc(skew_out, 16)
                            load(q, j, gu_d[f, 32 + 4 * (lq + 1) + j] if lq + 1 < 3
                                 else down2_d[f, 4 * (lq - 2) + j])
                        elif lq + 1 < 4:
                            load(q, j, gu_d[f, third * 16 + (4 * (lq + 1) + j)])
                        elif lq + 1 < 6:
                            load(q, j, down_d[f, third * 8 + (4 * (lq - 3) + j)])
                        else:
                            load(q, j, gu_d[f, third * 16 + (16 + j)])
                walk_ffn(sp, step)

            def projection(q0, n, src, after):
                with sp.Fori(1, n) as i:
                    for j in range(SLOTS):
                        load(q0 + i, j, src[i * 4 + j])
                for j in range(SLOTS):
                    if q0 == Q_OIN and j == 3:
                        sp.wait_ge(num_done, HC)
                    load(q0 + n, j, after[j])

            sp.dma_start(PAR[:], par_d).then_inc(par_in, 16)
            for j in range(SLOTS):
                sp.dma_start(X[:, 2 * j:2 * j + 2, :], xT[:, 2 * j:2 * j + 2, :]).then_inc(x_in[j], 16)
                if j == 0:
                    sp.dma_start(RAW[0][:], gu_d[0, 0]).then_inc(weights_in[0], 16)
            for j in range(1, SLOTS):
                sp.dma_start(RAW[j][:], gu_d[0, j]).then_inc(weights_in[j], 16)
            sp.dma_start(CST[:], cst_d).then_inc(cst_in, 16)
            sp.dma_start(RELB[:], relb_d).then_inc(hot_in, 16)
            sp.dma_start(HOT[:], hot_d).then_inc(hot_in, 16)
            sp.dma_start(POOLW[:], poolw_d).then_inc(prep_in, 16)
            sp.dma_start(PICK[:], pick_d).then_inc(prep_in, 16)
            sp.dma_start(W3[:], w3_d).then_inc(prep_in, 16)

            ffn(0, Q_FFN[0], ein_d)
            sp.wait_ge(skew_out, 16)
            for h in range(HA):
                flat = skew_d[h].rearrange("p z -> (p z)")
                skewed = flat[P - 1:P - 1 + P * (BW - 1)].rearrange("(p z) -> p z", z=BW - 1)[:, 0:T]
                sp.dma_start(G[:, h, :], skewed).then_inc(skew_in, 16)
            projection(Q_EIN, 4, ein_d, eout_d)
            projection(Q_EOUT, 2, eout_d, gu_d[1])
            ffn(1, Q_FFN[1], gu_d[2])
            sp.dma_start(WGR[:].rearrange("p a c o n -> p (a c o n)"), wgr_d).then_inc(prep_in, 16)
            ffn(2, Q_FFN[2], oin_d)
            projection(Q_OIN, 8, oin_d, oout_d)
            projection(Q_OOUT, 4, oout_d, gu_d[3])
            ffn(3, Q_FFN[3], None)
            for m in range(KX):
                sp.wait_ge(bank_free, 4 * Q_END - 8 + m + 5)
                sp.dma_start(out_d[:, m, :], X[:, m, :]).then_inc(out_done, 16)
            sp.wait_ge(out_done, 16 * KX)

        @block.tensor
        def _(pe):
            def unit(q, j, kt, hi, lo, order=None, ready=None, bank=None):
                bank = j if bank is None else bank
                pe.wait_ge(lo_ready, 4 * q + j + 1)
                pe.wait_ge(bank_free, 4 * q + j + 1)
                products(j, bank, order or list(range(kt)), 0, kt, hi, lo, ready)

            def products(j, bank, order, n0, n1, hi, lo, ready=None):
                for n in range(n0, n1):
                    k = order[n]
                    if ready:
                        ready(k)
                    c = slice(k * P, k * P + P)
                    pe.matmul(PS[bank][:], HI[j][:, c], hi(k), start=(n == 0), stop=False)
                    pe.matmul(PS[bank][:], HI[j][:, c], lo(k), start=False, stop=False)
                    last = pe.matmul(PS[bank][:], LO[j][:, c], hi(k), start=False, stop=(n == len(order) - 1))
                if n1 == len(order):
                    last.then_inc(unit_done, 1)

            def xh(k):
                return XH[:, k, :]

            def xl(k):
                return XL[:, k, :]

            def x_tile_ready(r):
                return lambda k: pe.wait_ge(xl_ready, 8 * r + k + 1)

            def two_units(q, ready):
                for n0, n1 in ((0, KX - 1), (KX - 1, KX)):
                    for j in range(2):
                        pe.wait_ge(lo_ready, 4 * q + j + 1)
                        pe.wait_ge(bank_free, 4 * q + j + 1)
                        products(j, j, list(range(KX)), n0, n1, xh, xl, ready if j == 0 else None)

            def norm(r):
                if r == 0:
                    pe.wait_ge(cst_in, 16)
                pe.wait_ge(sq_ready, 8 * r + 8)
                pe.matmul(AUX[:], ones, SQ[:], start=True, stop=True).then_inc(norm_sum, 1)

            def bias_table(h):
                if h == 0:
                    pe.wait_ge(bias_ready, 3)
                for part, (z0, z1) in enumerate(((0, T), (T, BW))):
                    n = 2 * h + part
                    if n >= 3:
                        pe.wait_ge(bias_staged, n - 2)
                    for w in (RBH, RBL):
                        last = pe.matmul(PS[5 + n % 3][:, 0:z1 - z0], w[:, h:h + 1].to_broadcast([P, P]),
                                         HOTR[:, z0:z1], start=(w is RBH), stop=(w is RBL))
                    last.then_inc(bias_sum, 1)

            def ffn(f, q0, r):
                unit(q0, 0, KX, xh, xl, ready=x_tile_ready(r))
                if f:
                    norm(r)

                def quad(q, third, lq, last, first=0):
                    for j in range(first, SLOTS):
                        if is_gate_up(lq, last):
                            unit(q, j, KX, xh, xl)
                            if q == 0 and j == 1:
                                norm(0)
                            if f == 0 and last and lq < 2:
                                bias_table(4 * lq + j)
                        else:
                            kt = 6 if last else 8
                            pair = 22 * f + 8 * third
                            tile_ready = (lambda k: pe.wait_ge(hl_ready, pair + (k + 1))) if j == 0 else None
                            unit(q, j, kt, lambda k: HH[:, k, :], lambda k: HL[:, k, :], ready=tile_ready)

                quad(q0, 0, 0, False, first=1)
                for lq in range(1, 6):
                    quad(q0 + lq, 0, lq, False)
                for lq in range(6):
                    quad(q0 + 6 + lq, 1, lq, False)
                for lq in range(5):
                    quad(q0 + 12 + lq, 2, lq, True)

            def even_mixer():
                q0 = Q_EIN
                two_units(q0, x_tile_ready(1))
                norm(1)
                for j in range(2, SLOTS):
                    unit(q0, j, KX, xh, xl)
                with pe.Fori(1, 3) as i:
                    for j in range(SLOTS):
                        unit(q0 + i, j, KX, xh, xl)
                for m in range(8):
                    pe.wait_ge(qk_sq, m + 1)
                    last = pe.matmul(PS[5][0:16, :], CST[:, K_HS + 16 * m:K_HS + 16 * m + 16], SQB[:, m, :],
                                     start=(m == 0), stop=(m == 7))
                last.then_inc(qk_rows, 1)
                for m in range(4):
                    if m >= 2:
                        pe.wait_ge(v_ready, m - 1)
                    pe.wait_ge(bank_free, 4 * (q0 + 2) + m + 5)
                    for j in range(TT):
                        last = pe.transpose(PS[6 + m % 2][:, j * P:j * P + P], TMP[:, m, j * P:j * P + P], ident)
                    last.then_inc(v_turned, 1)

                def spread(n):
                    m = (4, 5, 6, 7, 0, 1, 2, 3)[n]
                    if n == 0:
                        pe.wait_ge(row_lo, 1)
                        pe.wait_ge(pick_ready, 1)
                        pe.wait_ge(v_ready, 4)
                    if n >= 4:
                        pe.wait_ge(qk_normed, n - 3)
                    pe.matmul(PS[4 + n % 4][:], PICKR[:, m * P:m * P + P], ROWH[:], start=True, stop=False)
                    pe.matmul(PS[4 + n % 4][:], PICKR[:, m * P:m * P + P], ROWL[:], start=False,
                              stop=True).then_inc(qk_bcast, 1)

                for j in range(SLOTS):
                    unit(q0 + 3, j, KX, xh, xl)
                    for n in ((), (0, 1, 2, 3), (4, 5, 6, 7), ())[j]:
                        spread(n)

                def scores(a):
                    hp, i, half = ROWS[a]
                    n = (i + 1) * P
                    if i == 0 and half == 0:
                        pe.wait_ge(qk_normed, 4 + hp + 1)
                    if a >= 2:
                        pe.wait_ge(s_shift, a - 1)
                    else:
                        pe.wait_ge(bank_free, 4 * Q_EOUT + a + 1)
                    pe.matmul(PS[a % 2][:, 0:n], QZ[half][:, hp, i * P:i * P + P], QK[:, 4 + hp, 0:n],
                              start=True, stop=True).then_inc(s_done, 1)

                def turn(a):
                    _, i, _ = ROWS[a]
                    pe.wait_ge(p_ready, a + 1)
                    if a >= 2:
                        pe.wait_ge(pt_ready, a - 1)
                    else:
                        pe.wait_ge(bank_free, 4 * Q_EOUT + a + 3)
                    for j in range(i + 1):
                        last = pe.transpose(PS[2 + a % 2][:, j * P:j * P + P], TMP[:, 2 + a % 3, j * P:j * P + P],
                                            ident)
                    last.then_inc(pt_done, 1)

                def values(a):
                    hp, i, half = ROWS[a]
                    head = 2 * hp + half
                    pe.wait_ge(pt_ready, a + 1)
                    if a == 0:
                        pe.wait_ge(qk_normed, 8)
                    if i == 0 and half == 0 and hp >= 2:
                        pe.wait_ge(attn_lo, hp - 1)
                    for j in range(i + 1):
                        last = pe.matmul(PS[6 + hp % 2][64 * half:64 * half + 64, i * P:i * P + P],
                                         V[:, j, EA * head:EA * head + EA], TMP[:, 5 + a % 3, j * P:j * P + P],
                                         start=(j == 0), stop=(j == i))
                    last.then_inc(pv_done, 1)

                def pool_group(g):
                    pe.wait_ge(diff_ready, g + 1)
                    if g == 0:
                        pe.wait_ge(qk_normed, 8)
                    if g >= 2:
                        pe.wait_ge(pool_lo, g - 1)
                    pe.matmul(PS[4 + g % 2][:], POOLW[:, g, :], U[:, g, PAD:], start=True,
                              stop=True).then_inc(pool_mm, 1)

                for a in range(len(ROWS) + 3):
                    if a < len(ROWS):
                        scores(a)
                    if a in POOL_AT:
                        pool_group(POOL_AT[a])
                    if 2 <= a < len(ROWS) + 2:
                        turn(a - 2)
                    if a >= 3:
                        values(a - 3)

                def mixed_ready(k):
                    pe.wait_ge(pool_lo if k >= 4 else attn_lo, k % 4 + 1)

                for q in range(2):
                    for j in range(SLOTS):
                        unit(Q_EOUT + q, j, KX, lambda k: HH[:, k, :], lambda k: HL[:, k, :],
                             order=[4, 5, 6, 7, 0, 1, 2, 3], ready=mixed_ready if q == 0 and j == 0 else None)

            def odd_mixer():
                q0 = Q_OIN
                unit(q0, 0, KX, xh, xl, ready=x_tile_ready(4))
                norm(4)
                for j in range(1, SLOTS):
                    unit(q0, j, KX, xh, xl)
                def bank(item):
                    r = ITEM[item]
                    if r >= 3:
                        pe.wait_ge(item_read[r % 3], r // 3)
                    return PS[5 + r % 3]

                def joined(h):
                    pe.wait_ge(bd_ready, h + 1)
                    ps = bank((h, "A", 0))
                    for c in range(HT_):
                        last = pe.matmul(ps[:, c * P:c * P + P], (BD if h else BD0)[:, 0, c, :],
                                         (BD if h else BD0)[:, 1, c, :], start=True, stop=True)
                    last.then_inc(item_done, 1)

                for u in range(4, 2 * CT):
                    unit(q0 + u // 4, u % 4, KX, xh, xl)
                    m, z = u - GATE_UNIT, u - CT
                    for n, tile in ((2 * m, m), (2 * m + 1, CT + m)) if 0 <= m < CT else ():
                        if n == 0:
                            pe.wait_ge(wps_lo, 1)
                        pe.wait_ge(gate_lo, n + 1)
                        pe.matmul(AUX[0:4 * HC, :], WPS[:, tile, :], GXH[:, n % 2, :], start=(n == 0), stop=False)
                        pe.matmul(AUX[0:4 * HC, :], WPS[:, tile, :], GXL[:, n % 2, :], start=False,
                                  stop=(n == 2 * CT - 1)).then_inc(gate_sum, 1)
                    if z == 8:
                        pe.wait_ge(gate_rows, 1)
                        pe.matmul(PS[5][0:32 + HC, :], CST[:, K_SEL:K_SEL + 32 + HC], TMP[:, 2, :], start=True,
                                  stop=True).then_inc(fg_rows, 1)
                    if z == 13:
                        pe.wait_ge(a_rows, 1)
                        for j in range(TT):
                            last = pe.transpose(PS[6][:, HC * j:HC * j + HC], TMP[0:HC, 4, j * P:j * P + P],
                                                ident[0:HC, 0:HC])
                        last.then_inc(a_turned, 1)
                    if z == 14:
                        pe.wait_ge(m_rows, 1)
                        joined(0)

                def mean_square(h):
                    ps = bank((h, "ms", 0))
                    pe.wait_ge(ssq_step, 3 * h + 3)
                    pe.matmul(ps[:], ones, SQ[:], start=True, stop=True).then_inc(item_done, 1)

                pe.wait_ge(acol_ready, 1)
                for h in range(HC):
                    read_through(pe, (h, "A", 0))
                    for c in range(HT_):
                        ps = bank((h, "q", c))
                        pe.matmul(ps[:], (AM if h else AM0)[:, c, :], XC[:, HT_ * h + c, :], start=True,
                                  stop=True).then_inc(item_done, 1)
                    for c in range(HT_):
                        ps = bank((h, "v", c))
                        for j in range(TT):
                            last = pe.matmul(ps[:, j * P:j * P + P], XM[:, HT_ * h + c, j * P:j * P + P],
                                             (BD if h else BD0)[:, 2, c, :], start=True, stop=True)
                        last.then_inc(item_done, 1)
                        if h and c == 1:
                            mean_square(h - 1)
                        if h == 0 and c == 2:
                            pe.wait_ge(mem_lo, 1)
                            pe.wait_ge(sel_ready, 1)
                        pick = SELR[:, h:h + 1].to_broadcast([P, P])
                        for n, name in enumerate(("M", "EM")) if c == 2 else ():
                            ps = bank((h, name, 0))
                            pe.matmul(ps[:], pick, MEM[:, n, :], start=True, stop=True).then_inc(item_done, 1)
                    read_through(pe, (h, "q", HT_ - 1))
                    for j in range(TT):
                        ps = bank((h, "s", j))
                        for c in range(HT_):
                            last = pe.matmul(ps[:, 0:T - P * j], XC[:, HT_ * h + c, j * P:j * P + P], Q[:, c, j * P:],
                                             start=(c == 0), stop=(c == HT_ - 1))
                        last.then_inc(item_done, 1)
                    if h == 0:
                        pe.wait_ge(bank_free, 4 * Q_OOUT + 4)
                    one = SELR[:, HC:HC + 1].to_broadcast([P, P])
                    for j in range(TT):
                        pe.wait_ge(ptl_ready, TT * h + j + 1)
                        pth, ptl = PTH[:, PO[j]:PO[j + 1]], PTL[:, PO[j]:PO[j + 1]]
                        keys, end = slice(j * P, j * P + P), j == TT - 1
                        for c in range(HT_):
                            if h and j == 0:
                                pe.wait_ge(num_read, HT_ * (h - 1) + c + 1)
                            vh = VH[:, HT_ * h + c, keys]
                            pe.matmul(PS[c][:, j * P:], vh, pth, start=(j == 0), stop=False)
                            pe.matmul(PS[c][:, j * P:], vh, ptl, start=False, stop=False)
                            pe.matmul(PS[c][:, j * P:], VL[:, c, keys], pth, start=False, stop=end)
                        pe.matmul(PS[4][:, j * P:], one, pth, start=(j == 0), stop=False)
                        last = pe.matmul(PS[4][:, j * P:], one, ptl, start=False, stop=end)
                        if j == 1 and h + 1 < HC:
                            joined(h + 1)
                    last.then_inc(num_done, 1)

                def y_tile_ready(half):
                    return lambda k: pe.wait_ge(yl_ready, 8 * half + k + 1)

                for half in range(2):
                    for q in range(2):
                        first = half == 0 and q == 0
                        for j in range(SLOTS):
                            if first and j == 0:
                                pe.wait_ge(den_abs, HC)
                            if first and j == 3:
                                read_out(pe, (HC - 1, "ms", 0))
                            if half == 0 and q == 1 and j == 0:
                                pe.wait_ge(num_read, CT)
                            unit(Q_OOUT + 2 * half + q, j, KX, lambda k: YH[:, 8 * half + k, :],
                                 lambda k: YL[:, 8 * half + k, :], bank=OUT_BANKS[j] if first else None,
                                 ready=y_tile_ready(half) if q == 0 and j == 0 else None)
                            if first and j == 0:
                                mean_square(HC - 1)

            ffn(0, Q_FFN[0], 0)
            even_mixer()
            ffn(1, Q_FFN[1], 2)
            ffn(2, Q_FFN[2], 3)
            odd_mixer()
            ffn(3, Q_FFN[3], 5)

        @block.scalar
        def _(act):
            steps = [0]

            def link(ins):
                steps[0] += 1
                ins.then_inc(scalar_step, 1)
                act.wait_ge(scalar_step, steps[0])

            def split_hi(q, j, kt):
                act.wait_ge(weights_in[j], 16 * (q + 1))
                act.activation(HI[j][:, 0:kt * P], RAW[j][:, 0:kt * P], ACT.Copy).then_inc(hi_ready, 1)

            def gain_tile(r, m):
                act.activation(XH[:, m, :], X[:, m, :], ACT.Copy, scale=par(C_NORM + 8 * r + m)).then_inc(xh_ready, 1)

            def square_tile(r, m):
                if 8 * r + m >= 2:
                    act.wait_ge(sq_ready, 8 * r + m - 1)
                act.activation(GT[:, m % 2, :], X[:, m, :], ACT.Square).then_inc(sqt_ready, 1)

            def norm(r):
                act.wait_ge(norm_sum, r + 1)
                act.activation(RSTD[:], AUX[:], ACT.Sqrt, scale=1.0 / DM, bias=EPST[:]).then_inc(std_ready, 1)

            def residual_tile(q, j, r, m):
                if r is not None:
                    act.wait_ge(bank_free, 4 * q + j + 5)
                    gain_tile(r, m)
                    square_tile(r, m)

            def ffn(f, q0, r, after):
                def step(third, lq, last):
                    q = q0 + 6 * third + lq
                    for j in range(SLOTS):
                        if is_gate_up(lq, last):
                            m = 2 * lq + j // 2
                            act.wait_ge(bank_free, 4 * q + j + 5)
                            if j % 2 == 0:
                                act.activation(SG[:, m % 2, :], GT[:, m % 2, :], ACT.Silu).then_inc(silu_ready, 1)
                            else:
                                act.activation(HH[:, m, :], HT[:, m % 2, :], ACT.Copy).then_inc(hh_ready, 1)
                        elif last and after:
                            residual_tile(q, j, r, 4 * (lq - 3) + j)
                        if last and lq >= 2:
                            if lq < 4:
                                split_hi(q + 1, j, 6)
                            elif after:
                                split_hi(q + 1, j, 8)
                        else:
                            split_hi(q + 1, j, 8)
                        if f == 0 and last and lq < 2:
                            h = 4 * lq + j
                            for n, (z0, z1) in ((2 * h, (0, T)), (2 * h + 1, (T, BW))):
                                act.wait_ge(bias_sum, n + 1)
                                act.activation(STG[:, h, z0:z1], PS[5 + n % 3][:, 0:z1 - z0],
                                               ACT.Copy).then_inc(bias_staged, 1)
                walk_ffn(act, step)

            def even_mixer():
                act.wait_ge(prep_in, 48)
                act.activation(PICKR[:], PICK[:], ACT.Copy).then_inc(pick_ready, 1)
                for lq in range(4):
                    for j in range(SLOTS):
                        u = 4 * lq + j
                        if u < 8:
                            act.wait_ge(bank_free, 4 * (Q_EIN + lq) + j + 5)
                            act.activation(SQB[:, u, :], QK[:, u, :], ACT.Square).then_inc(qk_sq, 1)
                        if u == 12:
                            act.wait_ge(qk_rows, 1)
                            act.wait_ge(rows_clear, 1)
                            act.activation(TMP[0:16, 4, :], PS[5][0:16, :], ACT.Sqrt, scale=1.0 / EA,
                                           bias=EPST[0:16, :]).then_inc(row_std, 1)
                            for m in range(4):
                                act.wait_ge(v_turned, m + 1)
                                act.activation(V[:, 0:4, m * P:m * P + P],
                                               PS[6 + m % 2][:].rearrange("p (j f) -> p j f", j=TT),
                                               ACT.Copy).then_inc(v_ready, 1)
                        if u < 15:
                            split_hi(Q_EIN + lq + 1, j, 8)
                        if u == 12:
                            act.wait_ge(row_rstd, 1)
                            act.activation(ROWH[:], TMP[:, 4, :], ACT.Copy).then_inc(row_hi, 1)

                def exponentials(a):
                    _, i, _ = ROWS[a]
                    n = (i + 1) * P
                    act.wait_ge(s_shift, a + 1)
                    if a >= 3:
                        act.wait_ge(pt_done, a - 2)
                    act.activation(TMP[:, 2 + a % 3, 0:n], TMP[:, a % 2, 0:n], ACT.Exp, scale=-1.0,
                                   bias=ATT[:, 0, a:a + 1], accum_out=ATT[:, 1, a:a + 1]).then_inc(p_exp, 1)

                def turned(a):
                    _, i, _ = ROWS[a]
                    n = (i + 1) * P
                    act.wait_ge(pt_done, a + 1)
                    if a >= 3:
                        act.wait_ge(pv_done, a - 2)
                    act.activation(TMP[:, 5 + a % 3, 0:n], PS[2 + a % 2][:, 0:n], ACT.Copy).then_inc(pt_ready, 1)

                for a in range(len(ROWS) + 5):
                    if a < len(ROWS):
                        exponentials(a)
                    if a == 4:
                        split_hi(Q_EOUT, 3, 8)
                    if 2 <= a < len(ROWS) + 2:
                        turned(a - 2)
                    if a - 2 in POOL_AT:
                        g = POOL_AT[a - 2]
                        act.wait_ge(pool_mm, g + 1)
                        act.activation(HH[:, 4 + g, :], PS[4 + g % 2][:], ACT.Copy,
                                       scale=par(C_PSC + g)).then_inc(pool_hi, 1)
                    if a >= 12 and (a - 12) % 8 == 0:
                        hp = (a - 12) // 8
                        act.wait_ge(pv_done, 8 * hp + 8)
                        act.activation(HH[:, hp, :], PS[6 + hp % 2][:], ACT.Copy).then_inc(attn_hi, 1)
                for lq in range(2):
                    for j in range(SLOTS):
                        residual_tile(Q_EOUT + lq, j, 2, 4 * lq + j)
                        split_hi(Q_EOUT + lq + 1, j, 8)

            def odd_mixer():
                def silu_conv(c):
                    act.wait_ge(conv_step, 3 * c + 3)
                    act.activation(XC[:, c, :], XC[:, c, :], ACT.Silu).then_inc(xc_ready, 1)

                def gates():
                    act.wait_ge(gate_sum, 2 * CT)
                    act.wait_ge(mem_clear, 1)
                    act.activation(TMP[0:4 * HC, 2, :], AUX[0:4 * HC, :], ACT.Identity,
                                   bias=PAR[0:4 * HC, C_BG:C_BG + 1]).then_inc(gate_rows, 1)

                def log_sigmoid():
                    act.wait_ge(fg_rows, 1)
                    act.activation(TMP[0:HC, 3, :], PS[5][32:32 + HC, :], ACT.Abs).then_inc(fg_abs, 1)
                    act.wait_ge(fg_abs, 1)
                    link(act.activation(TMP[0:HC, 3, :], TMP[0:HC, 3, :], ACT.Exp, scale=-1.0))
                    act.activation(TMP[0:HC, 3, :], TMP[0:HC, 3, :], ACT.Ln, bias=ones[0:HC, 0:1]).then_inc(log_rows, 1)

                def read(h, name, c, out, **kw):
                    r = ITEM[(h, name, c)]
                    act.wait_ge(item_done, r + 1)
                    ins = act.activation(out, PS[5 + r % 3][:], ACT.Copy, **kw)
                    ins.then_inc(item_read[r % 3], 1)
                    return r

                act.wait_ge(cst_in, 16)
                act.activation(SELR[:], CST[:, K_ROW:K_ROW + HC + 1], ACT.Copy).then_inc(sel_ready, 1)
                for lq in range(8):
                    for j in range(SLOTS):
                        c = 4 * lq + j
                        act.wait_ge(bank_free, 4 * (Q_OIN + lq) + j + 5)
                        m = c + 1 - GATE_UNIT
                        for n in (2 * m, 2 * m + 1) if 0 <= m < CT else ():
                            if n >= 2:
                                act.wait_ge(gate_sum, n - 1)
                            act.wait_ge(xc_ready, m + 1)
                            act.activation(GXH[:, n % 2, :], (XM if n % 2 else XC)[:, m, :],
                                           ACT.Copy).then_inc(gate_hi, 1)
                        if c < CT:
                            if c == 13:
                                act.wait_ge(prep_ready, 2)
                            act.activation(XC[:, c, :], XM[:, c, :], ACT.Identity, scale=par(C_CONV + 3 * CT + c),
                                           bias=par(C_CONVB + c)).then_inc(tap0, 1)
                        else:
                            act.activation(SZ[:, c - CT, :], GT[:, c % 2, :], ACT.Silu).then_inc(sz_ready, 1)
                        if c < 2 * CT - 1:
                            split_hi(Q_OIN + lq + 1, j, 8)
                        if 1 <= c <= CT:
                            silu_conv(c - 1)
                        if c == 4:
                            act.wait_ge(prep_ready, 2)
                            act.activation(WPS[:, :, 0:8], WP[:], ACT.Copy).then_inc(wps_hi, 1)
                        if c == CT + 7:
                            gates()
                        if c == CT + 8:
                            log_sigmoid()
                        if c == CT + 14:
                            act.wait_ge(mem_lo, 1)
                            read(0, "A", 0, AM0[:], scale=EC ** -0.5)
                        if c == CT + 12:
                            act.wait_ge(m_rows, 1)
                            link(act.activation(TMP[0:HC, 3, :], TMP[0:HC, 3, :], ACT.Exp, scale=-1.0))
                            for n in range(2):
                                act.activation(MEM[0:HC, n, :], TMP[0:HC, 2 + n, :], ACT.Copy).then_inc(mem_hi, 1)

                def finish_y(h, tiles):
                    for c in tiles:
                        act.wait_ge(y_ready, HT_ * h + c + 1)
                        act.activation(YH[:, HT_ * h + c, :], TMP[:, 2 + c, :], ACT.Copy).then_inc(yh_ready, 1)

                def root(h):
                    read_out(act, (h, "ms", 0))
                    act.activation(RSTD[:], RSTD[:], ACT.Sqrt).then_inc(tstd_ready, 1)

                def square_numerator(h, c):
                    if c == 3:
                        act.wait_ge(ssq_step, 3 * h + 1)
                    act.activation((SQ[:], SQX[:], TMP[:, 6, :], SQX[:])[c], PS[c][:], ACT.Square).then_inc(num_sq, 1)

                for h in range(HC):
                    for c in range(HT_):
                        if h:
                            square_numerator(h - 1, c)
                        read(h, "q", c, Q[:, c, :])
                    for c in range(HT_):
                        r = ITEM[(h, "v", c)]
                        act.wait_ge(item_done, r + 1)
                        act.activation(VH[:, HT_ * h + c, :], PS[5 + r % 3][:], ACT.Copy).then_inc(vh_ready, 1)
                        if c == 2:
                            read(h, "M", 0, TMP[:, 6, :])
                            if h:
                                root(h - 1)
                    if h >= 2:
                        finish_y(h - 2, (2, 3))
                    read_out(act, (h, "M", 0))
                    for j in range(TT + 2):
                        if j >= 2:
                            read_out(act, (h, "s", j - 2))
                            act.activation(PTH[:, PO[j - 2]:PO[j - 1]], TMP[:, j % 2, 0:T - P * (j - 2)],
                                           ACT.Copy).then_inc(pth_ready, 1)
                        if j == TT or j == TT + 1:
                            continue
                        n = TT * h + j
                        if n >= 2:
                            act.wait_ge(ptl_ready, n - 1)
                        act.activation(TMP[:, j % 2, 0:T - P * j], TMP[:, 6, j * P:], ACT.Exp, scale=-1.0,
                                       bias=ACOL[:, j, h:h + 1]).then_inc(wt_exp, 1)
                    if h + 1 < HC:
                        read(h + 1, "A", 0, AM[:], scale=EC ** -0.5)
                    if h:
                        finish_y(h - 1, (0, 1))
                    act.wait_ge(num_done, h + 1)
                    act.activation(RSTD[:], PS[4][:], ACT.Abs).then_inc(den_abs, 1)
                for c in range(HT_):
                    square_numerator(HC - 1, c)
                finish_y(HC - 2, (2, 3))
                root(HC - 1)
                split_hi(Q_OOUT, 3, 8)
                for lq in range(4):
                    for j in range(SLOTS):
                        residual_tile(Q_OOUT + lq, j, 5 if lq >= 2 else None, 4 * (lq % 2) + j)
                        split_hi(Q_OOUT + lq + 1, j, 8)
                        if lq == 0:
                            finish_y(HC - 1, (j,))

            act.wait_ge(small_ready, 1)
            act.activation(ATT[:, 0, 0:1], EPST[:], ACT.Copy)
            act.wait_ge(par_in, 16)
            split_hi(0, 0, 8)
            for m in range(KX):
                act.wait_ge(x_in[m // 2], 16)
                gain_tile(0, m)
            for m in range(KX):
                if m in (0, 5):
                    split_hi(0, 1 if m == 0 else 2, 8)
                square_tile(0, m)
            split_hi(0, 3, 8)
            act.wait_ge(hot_in, 32)
            act.activation(HOTR[:], HOT[:], ACT.Copy).then_inc(bias_ready, 1)
            act.activation(RBH[:], RELB[:], ACT.Copy).then_inc(bias_ready, 1)
            norm(0)
            ffn(0, Q_FFN[0], 1, True)
            norm(1)
            even_mixer()
            norm(2)
            ffn(1, Q_FFN[1], 3, True)
            norm(3)
            ffn(2, Q_FFN[2], 4, True)
            norm(4)
            odd_mixer()
            norm(5)
            ffn(3, Q_FFN[3], None, False)

        @block.vector
        def _(dve):
            steps = [0]

            def link(ins):
                steps[0] += 1
                ins.then_inc(vector_step, 1)
                dve.wait_ge(vector_step, steps[0])

            def split_lo(q, j, kt):
                dve.wait_ge(hi_ready, 4 * q + j + 1)
                dve.tensor_tensor(LO[j][:, 0:kt * P], RAW[j][:, 0:kt * P], HI[j][:, 0:kt * P].bitcast(F32),
                                  ALU.subtract).then_inc(lo_ready, 1)

            def new_x_tile(r, m):
                dve.wait_ge(xh_ready, 8 * r + m + 1)
                dve.scalar_tensor_tensor(XL[:, m, :], X[:, m, :], par(C_NORM + 8 * r + m), XH[:, m, :].bitcast(F32),
                                         ALU.mult, ALU.subtract).then_inc(xl_ready, 1)

            def norm(r):
                dve.wait_ge(std_ready, r + 1)
                dve.reciprocal(RSTD[:], RSTD[:]).then_inc(rstd_ready, 1)
                dve.wait_ge(rstd_ready, r + 1)

            def scaled(q, j, out):
                dve.wait_ge(unit_done, 4 * q + j + 1)
                dve.tensor_tensor(out, PS[j][:], RSTD[:], ALU.mult).then_inc(bank_free, 1)

            def residual_tile(q, j, r, m, factor, bank=None):
                dve.wait_ge(unit_done, 4 * q + j + 1)
                dve.scalar_tensor_tensor(X[:, m, :], PS[j if bank is None else bank][:], factor, X[:, m, :], ALU.mult,
                                         ALU.add).then_inc(bank_free, 1)
                if r is not None:
                    new_x_tile(r, m)

            def ffn(f, q0, r, after):
                def step(third, lq, last):
                    q = q0 + 6 * third + lq
                    for j in range(SLOTS):
                        if is_gate_up(lq, last):
                            m = 2 * lq + j // 2
                            if j % 2 == 0:
                                scaled(q, j, GT[:, m % 2, :])
                            else:
                                dve.wait_ge(sr_ready, 22 * f + 8 * third + (m + 1))
                                dve.wait_ge(unit_done, 4 * q + j + 1)
                                dve.tensor_tensor(HT[:, m % 2, :], PS[j][:], SR[:, m % 2, :],
                                                  ALU.mult).then_inc(bank_free, 1)
                        else:
                            residual_tile(q, j, r if last else None, 4 * (lq - (3 if last else 4)) + j, 0.5)
                        if last and lq >= 2:
                            if lq < 4:
                                split_lo(q + 1, j, 6)
                            elif after:
                                split_lo(q + 1, j, 8)
                        else:
                            split_lo(q + 1, j, 8)
                walk_ffn(dve, step)

            def even_mixer():
                def norm_q(n):
                    dve.wait_ge(qk_bcast, n + 1)
                    for half in range(2):
                        h = slice(EA * half, EA * half + EA)
                        last = dve.scalar_tensor_tensor(QZ[half][h, n - 4, :], QK[h, n - 4, :], QG[h, :], PS[n][h, :],
                                                        ALU.mult, ALU.mult)
                    last.then_inc(qk_normed, 1)

                for lq in range(4):
                    for j in range(SLOTS):
                        u = 4 * lq + j
                        if u == 12:
                            dve.wait_ge(row_std, 1)
                            dve.reciprocal(TMP[0:16, 4, :], TMP[0:16, 4, :]).then_inc(row_rstd, 1)
                        scaled(Q_EIN + lq, j, QK[:, u, :] if u < 8 else TMP[:, u - 8, :] if u < 12
                               else U[:, u - 12, PAD:])
                        if u < 14:
                            split_lo(Q_EIN + lq + 1, j, 8)
                        if u == 12:
                            dve.wait_ge(row_hi, 1)
                            dve.tensor_tensor(ROWL[:], TMP[:, 4, :], ROWH[:].bitcast(F32),
                                              ALU.subtract).then_inc(row_lo, 1)
                        if u == 13:
                            for n in range(4):
                                dve.wait_ge(qk_bcast, n + 1)
                                dve.scalar_tensor_tensor(QK[:, 4 + n, :], QK[:, 4 + n, :], par(C_KG),
                                                         PS[4 + n][:], ALU.mult, ALU.mult).then_inc(qk_normed, 1)
                            dve.wait_ge(qz_clear, 2)
                        if u == 14:
                            norm_q(4)
                            norm_q(5)
                            split_lo(Q_EIN + lq + 1, j, 8)

                def shifted(a):
                    hp, i, half = ROWS[a]
                    n = (i + 1) * P
                    dve.wait_ge(s_done, a + 1)
                    if a >= 2:
                        dve.wait_ge(p_exp, a - 1)
                    else:
                        dve.wait_ge(v_turned, 4)
                    dve.tensor_tensor_reduce(TMP[:, a % 2, 0:n], PS[a % 2][:, 0:n],
                                             G[:, 2 * hp + half, T - n:T], -1.0, 3.0e38, ALU.add, ALU.min,
                                             ATT[:, 0, a:a + 1]).then_inc(s_shift, 1)

                def normed(a):
                    _, i, _ = ROWS[a]
                    n = (i + 1) * P
                    dve.wait_ge(p_exp, a + 1)
                    dve.reciprocal(ATT[:, 2, a:a + 1], ATT[:, 1, a:a + 1]).then_inc(p_inv, 1)
                    dve.wait_ge(p_inv, a + 1)
                    dve.tensor_scalar(TMP[:, 2 + a % 3, 0:n], TMP[:, 2 + a % 3, 0:n], ATT[:, 2, a:a + 1], None,
                                      ALU.mult).then_inc(p_ready, 1)

                dve.wait_ge(skew_in, 16 * HA)
                for a in range(len(ROWS) + 6):
                    if a < len(ROWS):
                        shifted(a)
                    if a == 5:
                        split_lo(Q_EOUT, 3, 8)
                    if 1 <= a <= len(ROWS):
                        normed(a - 1)
                    if 1 <= a <= 2:
                        norm_q(5 + a)
                    if a - 3 in POOL_AT:
                        g = POOL_AT[a - 3]
                        dve.wait_ge(pool_hi, g + 1)
                        dve.scalar_tensor_tensor(HL[:, 4 + g, :], PS[4 + g % 2][:], par(C_PSC + g),
                                                 HH[:, 4 + g, :].bitcast(F32), ALU.mult,
                                                 ALU.subtract).then_inc(pool_lo, 1)
                    if a >= 13 and (a - 13) % 8 == 0:
                        hp = (a - 13) // 8
                        dve.wait_ge(attn_hi, hp + 1)
                        dve.tensor_tensor(HL[:, hp, :], PS[6 + hp % 2][:], HH[:, hp, :].bitcast(F32),
                                          ALU.subtract).then_inc(attn_lo, 1)
                for lq in range(2):
                    for j in range(SLOTS):
                        residual_tile(Q_EOUT + lq, j, 2, 4 * lq + j, 1.0)
                        split_lo(Q_EOUT + lq + 1, j, 8)

            def odd_mixer():
                def conv(c):
                    dve.wait_ge(tap0, c + 1)
                    for n, back in enumerate((1, 2, 3)):
                        if n:
                            dve.wait_ge(conv_step, 3 * c + n)
                        dve.scalar_tensor_tensor(XC[:, c, back:], XM[:, c, 0:T - back],
                                                 par(C_CONV + (TAPS - 1 - back) * CT + c), XC[:, c, back:],
                                                 ALU.mult, ALU.add).then_inc(conv_step, 1)

                def gate_rows_m():
                    fg, la = TMP[0:HC, 3, :], TMP[0:HC, 4, :]
                    dve.wait_ge(fg_abs, 1)
                    link(dve.tensor_scalar(la, PS[5][32:32 + HC, :], 0.0, None, ALU.min))
                    dve.wait_ge(log_rows, 1)
                    link(dve.tensor_tensor(la, la, fg, ALU.subtract))
                    link(dve.tensor_tensor_scan(fg, ones[0:HC, 0:1].to_broadcast([HC, T]), la, 0.0, ALU.mult,
                                                ALU.add))
                    dve.tensor_tensor(la, PS[5][0:HC, :], fg, ALU.subtract).then_inc(a_rows, 1)
                    dve.wait_ge(a_rows, 1)
                    link(dve.tensor_tensor_scan(TMP[0:HC, 2, :], la, la, 0.0, ALU.max, ALU.max))
                    dve.tensor_tensor(fg, fg, TMP[0:HC, 2, :], ALU.add).then_inc(m_rows, 1)

                for lq in range(8):
                    for j in range(SLOTS):
                        c = 4 * lq + j
                        if c >= CT + 2:
                            dve.wait_ge(sz_ready, c - CT - 1)
                        scaled(Q_OIN + lq, j, XM[:, c, :] if c < CT else GT[:, c % 2, :])
                        if 1 <= c <= CT:
                            conv(c - 1)
                        if c < 2 * CT - 1:
                            split_lo(Q_OIN + lq + 1, j, 8)
                        if c == CT + 9:
                            gate_rows_m()
                        if c == CT + 13:
                            for n in range(2):
                                dve.wait_ge(mem_hi, n + 1)
                                last = dve.tensor_tensor(MEM[32:32 + HC, n, :], TMP[0:HC, 2 + n, :],
                                                         MEM[0:HC, n, :].bitcast(F32), ALU.subtract)
                            last.then_inc(mem_lo, 1)
                            dve.wait_ge(a_turned, 1)
                            dve.tensor_copy(ACOL[:].rearrange("p j h -> p (j h)"),
                                            PS[6][:, 0:TT * HC]).then_inc(acol_ready, 1)

                def item(h, name, c):
                    r = ITEM[(h, name, c)]
                    dve.wait_ge(item_done, r + 1)
                    return PS[5 + r % 3], item_read[r % 3]

                def squares(h):
                    dve.wait_ge(den_abs, h + 1)
                    link(dve.tensor_tensor(RSTD[:], RSTD[:], TMP[:, 7, :], ALU.max))
                    link(dve.scalar_tensor_tensor(RSTD[:], RSTD[:], EPS, RSTD[:], ALU.mult, ALU.mult))
                    for n, other in enumerate((SQX[:], TMP[:, 6, :], SQX[:])):
                        dve.wait_ge(num_sq, 4 * h + n + 2)
                        if n:
                            dve.wait_ge(ssq_step, 3 * h + n)
                        dve.tensor_tensor(SQ[:], SQ[:], other, ALU.add).then_inc(ssq_step, 1)

                def head_factor(h):
                    ps, read = item(h, "ms", 0)
                    dve.scalar_tensor_tensor(RSTD[:], ps[:], 1.0 / EC, RSTD[:], ALU.mult, ALU.add).then_inc(read, 1)

                def invert_factor(h):
                    dve.wait_ge(tstd_ready, h + 1)
                    link(dve.reciprocal(RSTD[:], RSTD[:]))

                def scale_numerator(h):
                    for c in range(HT_):
                        if h:
                            dve.wait_ge(yl_ready, HT_ * (h - 1) + c + 1)
                        dve.scalar_tensor_tensor(TMP[:, 2 + c, :], PS[c][:], par(C_GAIN + HT_ * h + c), RSTD[:],
                                                 ALU.mult, ALU.mult).then_inc(num_read, 1)

                def add_skip(h):
                    for c in range(HT_):
                        ch = HT_ * h + c
                        dve.wait_ge(num_read, ch + 1)
                        dve.scalar_tensor_tensor(TMP[:, 2 + c, :], XC[:, ch, :], par(C_SKIP + ch), TMP[:, 2 + c, :],
                                                 ALU.mult, ALU.add).then_inc(y_pre, 1)

                for h in range(HC):
                    if h:
                        squares(h - 1)
                    for c in range(HT_):
                        ps, read = item(h, "v", c)
                        dve.wait_ge(vh_ready, HT_ * h + c + 1)
                        dve.tensor_tensor(VL[:, c, :], ps[:], VH[:, HT_ * h + c, :].bitcast(F32),
                                          ALU.subtract).then_inc(read, 1)
                        if h and c == 1:
                            head_factor(h - 1)
                        if c == 2:
                            ps, read = item(h, "EM", 0)
                            if h == 0:
                                item(0, "v", 3)
                            dve.tensor_copy(TMP[:, 7, :], ps[:]).then_inc(read, 1)
                    if h:
                        invert_factor(h - 1)

                    def weighted_lo(j):
                        dve.wait_ge(pth_ready, TT * h + j + 1)
                        dve.tensor_tensor(PTL[:, PO[j]:PO[j + 1]], TMP[:, j % 2, 0:T - P * j],
                                          PTH[:, PO[j]:PO[j + 1]].bitcast(F32), ALU.subtract).then_inc(ptl_ready, 1)

                    for j in range(TT):
                        dve.wait_ge(wt_ready, TT * h + j + 1)
                        ps, read = item(h, "s", j)
                        weights = TMP[:, j % 2, 0:T - P * j]
                        dve.tensor_tensor(weights, ps[:, 0:T - P * j], weights, ALU.mult).then_inc(read, 1)
                        if j:
                            weighted_lo(j - 1)
                        if h and j == 1:
                            scale_numerator(h - 1)
                    weighted_lo(TT - 1)
                    if h:
                        add_skip(h - 1)
                squares(HC - 1)
                head_factor(HC - 1)
                invert_factor(HC - 1)
                scale_numerator(HC - 1)
                split_lo(Q_OOUT, 3, 8)
                add_skip(HC - 1)
                for lq in range(4):
                    for j in range(SLOTS):
                        residual_tile(Q_OOUT + lq, j, 5 if lq >= 2 else None, 4 * (lq % 2) + j, 1.0,
                                      OUT_BANKS[j] if lq == 0 else None)
                        split_lo(Q_OOUT + lq + 1, j, 8)

            dve.memset(EPST[:], EPS).then_inc(small_ready, 1)
            dve.wait_ge(par_in, 16)
            dve.tensor_scalar(QG[:], par(C_QG), EA ** -0.5, None, ALU.mult).then_inc(bank_free, SLOTS)
            split_lo(0, 0, 8)
            for m in range(KX):
                new_x_tile(0, m)
            for m in range(KX):
                if m in (0, 5):
                    split_lo(0, 1 if m == 0 else 2, 8)
                dve.wait_ge(sqt_ready, m + 1)
                if m:
                    dve.wait_ge(sq_ready, m)
                    dve.tensor_tensor(SQ[:], SQ[:], GT[:, m % 2, :], ALU.add).then_inc(sq_ready, 1)
                else:
                    dve.tensor_copy(SQ[:], GT[:, 0, :]).then_inc(sq_ready, 1)
            split_lo(0, 3, 8)
            dve.wait_ge(bias_ready, 2)
            dve.tensor_tensor(RBL[:], RELB[:], RBH[:].bitcast(F32), ALU.subtract).then_inc(bias_ready, 1)
            norm(0)
            ffn(0, Q_FFN[0], 1, True)
            norm(1)
            even_mixer()
            norm(2)
            ffn(1, Q_FFN[1], 3, True)
            norm(3)
            ffn(2, Q_FFN[2], 4, True)
            norm(4)
            odd_mixer()
            norm(5)
            ffn(3, Q_FFN[3], None, False)

        @block.gpsimd
        def _(pool):
            steps = [0]

            def link(ins):
                steps[0] += 1
                ins.then_inc(pool_step, 1)
                pool.wait_ge(pool_step, steps[0])

            def square_tile(r, m):
                pool.wait_ge(sqt_ready, 8 * r + m + 1)
                if m:
                    pool.wait_ge(sq_ready, 8 * r + m)
                    pool.tensor_tensor(SQ[:], SQ[:], GT[:, m % 2, :], ALU.add).then_inc(sq_ready, 1)
                else:
                    pool.tensor_copy(SQ[:], GT[:, 0, :]).then_inc(sq_ready, 1)

            def ffn(f, q0, r):
                def step(third, lq, last):
                    if is_gate_up(lq, last):
                        for m in (2 * lq, 2 * lq + 1):
                            pair = 22 * f + 8 * third + (m + 1)
                            pool.wait_ge(silu_ready, pair)
                            pool.tensor_tensor(SR[:, m % 2, :], SG[:, m % 2, :], RSTD[:],
                                               ALU.mult).then_inc(sr_ready, 1)
                            pool.wait_ge(hh_ready, pair)
                            pool.tensor_tensor(HL[:, m, :], HT[:, m % 2, :], HH[:, m, :].bitcast(F32),
                                               ALU.subtract).then_inc(hl_ready, 1)
                    elif last and r is not None:
                        for j in range(SLOTS):
                            square_tile(r, 4 * (lq - 3) + j)
                walk_ffn(pool, step)

            def pool_group(g):
                pool.wait_ge(bank_free, 4 * (Q_EIN + 3) + g + 5)
                x = U[:, g, :]
                width, src = 1, x
                for n in range(g + 1):
                    dst = WSUM[:, n % 2, :]
                    link(pool.tensor_tensor(dst[:, PAD:], src[:, PAD:], src[:, PAD - width:PAD + T - width], ALU.add))
                    width, src = 2 * width, dst
                mean = src[:, PAD:]
                link(pool.tensor_scalar(mean, mean, 1.0 / WINDOWS[g], None, ALU.mult))
                link(pool.tensor_tensor(mean[:, 0:16], mean[:, 0:16], CST[:, K_FIX + 16 * g:K_FIX + 16 * g + 16],
                                        ALU.mult))
                pool.tensor_tensor(x[:, PAD:], mean, x[:, PAD:], ALU.subtract).then_inc(diff_ready, 1)
                pool.wait_ge(diff_ready, g + 1)

            def gate_weights():
                pool.wait_ge(prep_in, 64)
                flat = [CT, 4, 2 * HC]
                for t in range(3):
                    last = pool.tensor_tensor(WGR[:, t], WGR[:, t], W3[:, t].unsqueeze(3).to_broadcast([P] + flat),
                                              ALU.mult)
                link(last)
                link(pool.tensor_tensor(WGR[:, 0], WGR[:, 0], WGR[:, 1], ALU.add))
                for n, t in enumerate((0, 2)):
                    out = WP[:, n * CT:(n + 1) * CT, :]
                    link(pool.tensor_tensor(out, WGR[:, t, :, 0, :], WGR[:, t, :, 1, :], ALU.add))
                    link(pool.tensor_tensor(out, out, WGR[:, t, :, 2, :], ALU.add))
                    pool.tensor_tensor(out, out, WGR[:, t, :, 3, :], ALU.add).then_inc(prep_ready, 1)

            def block_diagonals(h):
                if h:
                    pool.wait_ge(item_done, ITEM[(h - 1, "v", HT_ - 1)] + 1)
                mask = CST[:, K_MASK:K_MASK + 32].unsqueeze(1).unsqueeze(3).to_broadcast([P, HT_, 32, 4])
                for t in range(3):
                    w = W3[:, (3, 4, 2)[t], HT_ * h:HT_ * h + HT_, :].unsqueeze(2).to_broadcast([P, HT_, 32, 4])
                    out = (BD if h else BD0)[:, t].rearrange("p c (g o) -> p c g o", g=32)
                    last = pool.tensor_tensor(out, w, mask, ALU.mult)
                last.then_inc(bd_ready, 1)

            def outputs(h):
                for c in range(HT_):
                    n = HT_ * h + c
                    pool.wait_ge(y_pre, n + 1)
                    pool.wait_ge(sz_ready, n + 1)
                    pool.tensor_tensor(TMP[:, 2 + c, :], TMP[:, 2 + c, :], SZ[:, n, :], ALU.mult).then_inc(y_ready, 1)
                for c in range(HT_):
                    n = HT_ * h + c
                    pool.wait_ge(yh_ready, n + 1)
                    pool.tensor_tensor(YL[:, n, :], TMP[:, 2 + c, :], YH[:, n, :].bitcast(F32),
                                       ALU.subtract).then_inc(yl_ready, 1)

            pool.memset(U[:, :, 0:PAD], 0.0)
            link(pool.memset(WSUM[:, :, 0:PAD], 0.0))
            ffn(0, Q_FFN[0], 1)
            pool.memset(TMP[:, 4, :], 0.0).then_inc(rows_clear, 1)
            pool.wait_ge(unit_done, 4 * Q_EIN)
            for half in range(2):
                pool.memset(QZ[half][:], 0.0).then_inc(qz_clear, 1)
            for g in range(NG):
                pool_group(g)
            for m in range(KX):
                square_tile(2, m)
            ffn(1, Q_FFN[1], 3)
            ffn(2, Q_FFN[2], 4)
            gate_weights()
            pool.memset(MEM[:].bitcast(F32), 0.0)
            pool.wait_ge(wps_hi, 1)
            pool.wait_ge(prep_ready, 2)
            pool.tensor_tensor(WPS[:, :, 8:16], WP[:], WPS[:, :, 0:8].bitcast(F32), ALU.subtract).then_inc(wps_lo, 1)
            for n in range(2 * CT):
                pool.wait_ge(gate_hi, n + 1)
                pool.tensor_tensor(GXL[:, n % 2, :], (XM if n % 2 else XC)[:, n // 2, :],
                                   GXH[:, n % 2, :].bitcast(F32), ALU.subtract).then_inc(gate_lo, 1)
            pool.wait_ge(gate_sum, 2 * CT)
            pool.memset(TMP[:, 2, :], 0.0).then_inc(mem_clear, 1)
            block_diagonals(0)
            for h in range(HC):
                for j in range(TT):
                    n = TT * h + j
                    pool.wait_ge(wt_exp, n + 1)
                    pool.affine_select(TMP[:, j % 2, 0:P], TMP[:, j % 2, 0:P], pattern=[[1, P]],
                                       compare_op=ALU.is_ge, fill=0.0, base=0,
                                       channel_multiplier=-1).then_inc(wt_ready, 1)
                if h + 1 < HC:
                    block_diagonals(h + 1)
                if h:
                    outputs(h - 1)
            outputs(HC - 1)
            for m in range(KX):
                square_tile(5, m)
            ffn(3, Q_FFN[3], None)



def tiles(w):
    i, o = w.shape
    return w.reshape(i // P, P, o // P, P).transpose(2, 1, 0, 3).reshape(o // P, P, (i // P) * P)


def lay_out(a):
    w = {}
    w["xT"] = a["x"][0].T.reshape(KX, P, T).transpose(1, 0, 2)
    gate, up, down = (a[n].reshape((NFFN,) + a[n].shape[2:]) for n in ("ffn_w_gate", "ffn_w_up", "ffn_w_down"))
    w["gu"] = np.stack([np.stack([tiles(gate[f]), tiles(up[f])], 1).reshape(2 * FT, P, KMAX * P) for f in range(NFFN)])
    w["down"] = np.stack([np.concatenate([tiles(down[f][t * 1024:t * 1024 + 1024]) for t in range(2)])
                          for f in range(NFFN)])
    w["down2"] = np.stack([tiles(down[f][2048:]) for f in range(NFFN)])
    w["ein"] = tiles(a["ev_w_in"][0])
    w["eout"] = tiles(a["ev_w_out"][0])
    w["oin"] = tiles(a["od_w_in"][0])
    w["oout"] = np.concatenate([tiles(a["od_w_out"][0][t * 1024:t * 1024 + 1024]) for t in range(2)])
    column = lambda v: v.reshape(-1, P).T
    bias = np.zeros((P, 1), np.float32)
    bias[0:2 * HC, 0] = a["od_b_gates"][0]
    w["par"] = np.concatenate([
        a["norm_gains"].reshape(6, KX, P).transpose(2, 0, 1).reshape(P, 48),
        a["od_conv_w"][0].reshape(TAPS, CT, P).transpose(2, 0, 1).reshape(P, TAPS * CT),
        column(a["od_conv_b"][0]), column(a["od_skip"][0]), column(a["od_out_gain"][0]), column(a["ev_pool_scale"][0]),
        np.tile(a["ev_q_gain"][0], 2)[:, None], np.tile(a["ev_k_gain"][0], 2)[:, None], bias], 1)
    w["cst"], w["hot"], w["pick"] = shape_constants()
    w["relb"] = np.concatenate([a["rel_bias"], np.ones((2, HA), np.float32),
                                np.zeros((P - BUCKETS - 2, HA), np.float32)])
    blocks = [a[n][0] for n in ("od_wq", "od_wk", "od_wv")] + [a[n][0].transpose(0, 2, 1) for n in ("od_wq", "od_wk")]
    w["w3"] = np.stack([b.reshape(CT, P, 4).transpose(1, 0, 2) for b in blocks], 1)
    gates = a["od_w_gates"][0].reshape(3, CT, P // 4, 1, 4, 2 * HC)
    w["wgr"] = np.broadcast_to(gates, (3, CT, P // 4, 4, 4, 2 * HC)).transpose(2, 3, 0, 1, 4, 5).reshape(P, -1)
    w["poolw"] = a["ev_pool_w"][0].transpose(1, 0, 2)
    return {n: np.ascontiguousarray(v) for n, v in w.items()}


def kernel(**inputs):
    import concourse.bacc as bacc
    from concourse.bass_utils import run_bass_kernel_spmd

    w = lay_out({n: np.asarray(v) for n, v in inputs.items()})
    nc = bacc.Bacc("TRN2", target_bir_lowering=False, num_devices=1)
    names = ["xT", "par", "cst", "hot", "relb", "w3", "wgr", "poolw", "pick", "gu", "down", "down2", "ein", "eout",
             "oin", "oout"]
    arrays = {n + "_dram": w[n] for n in names}
    args = [nc.dram_tensor(n + "_dram", w[n].shape, F32, kind="ExternalInput").ap() for n in names]
    args.append(nc.dram_tensor("skew_dram", (HA, P, BW), F32, kind="Internal").ap())
    args.append(nc.dram_tensor("out_dram", (P, KX, T), F32, kind="ExternalOutput").ap())
    trunk(nc, *args)
    r = run_bass_kernel_spmd(nc, [arrays], core_ids=[0])
    out = r.results[0]["out_dram"]
    return out.transpose(1, 0, 2).reshape(DM, T).T.reshape(1, T, DM)
```
